# Optimizing a Trainium2 kernel written in Bass

```python
import math
import jax
import jax.numpy as jnp
from jax import lax
import numpy as np

D_MODEL = 1024
BATCH = 1
SEQ = 256
DEPTH = 4
DEC_BATCH = 8
DEC_SEQ = 1
PAST_LEN = 1024
PAGE_SIZE = 128

N_MIXERS = 3
N_LAYERS_NSA = (DEPTH + 2) // 3
N_LAYERS_HGRN = (DEPTH + 1) // 3
N_LAYERS_SSD = DEPTH // 3

ADA_CHUNKS = 6
NORM_EPS = 1e-6
D_FF = 4 * D_MODEL

NSA_HEADS = 16
NSA_HEAD_DIM = D_MODEL // NSA_HEADS
NSA_KV_HEADS = 4
NSA_GROUP = NSA_HEADS // NSA_KV_HEADS
CMP_STRIDE = 16
CMP_LEN = 2 * CMP_STRIDE
CMP_HIDDEN = 2 * NSA_HEAD_DIM
SEL_BLOCK = 64
SEL_TOP_N = 16
WINDOW = 512
WIN_Q_BLOCK = 128
SEL_Q_BLOCK = 16
NSA_Q_W = NSA_HEADS * NSA_HEAD_DIM
NSA_KV_W = NSA_KV_HEADS * NSA_HEAD_DIM
NSA_IN_W = NSA_Q_W + 6 * NSA_KV_W + 3 * NSA_HEADS

REL_BUCKETS = 32
REL_MAX_DIST = 128

HG_EXPAND = 128
HG_HEADS = D_MODEL // HG_EXPAND
HG_DK = HG_EXPAND
HG_DV = D_MODEL // HG_HEADS
HG_CHUNK = 64
HG_IN_W = 2 * HG_HEADS * HG_DK + 2 * HG_HEADS * HG_DV

SSD_D_INNER = 2 * D_MODEL
SSD_HEAD_DIM = 64
SSD_HEADS = SSD_D_INNER // SSD_HEAD_DIM
SSD_GROUPS = 8
SSD_HPG = SSD_HEADS // SSD_GROUPS
SSD_STATE = 128
SSD_CONV_W = 4
SSD_CONV_DIM = SSD_D_INNER + 2 * SSD_GROUPS * SSD_STATE
SSD_IN_W = SSD_D_INNER + SSD_CONV_DIM + SSD_HEADS
SSD_CHUNK = 128

NEG_INF = -1e30
FORCE_SCORE = 1e4

kernel_name = 'hybrid_nsa_hgrn2_ssd_step'

def _rmsnorm(x, g):
    x32 = x.astype(jnp.float32)
    y = x32 * lax.rsqrt(jnp.mean(x32 * x32, axis=-1, keepdims=True) + NORM_EPS)
    return (y * g.astype(jnp.float32)).astype(x.dtype)

def _masked_softmax(logits, mask):
    l = jnp.where(mask, logits.astype(jnp.float32), NEG_INF)
    m = jnp.max(l, axis=-1, keepdims=True)
    e = jnp.where(mask, jnp.exp(l - m), 0.0)
    return e / jnp.maximum(jnp.sum(e, axis=-1, keepdims=True), 1e-30)

def _rel_bucket(dist):
    n = jnp.maximum(dist, 0)
    n_exact = REL_BUCKETS // 2
    nf = jnp.maximum(n, 1).astype(jnp.float32)
    large = n_exact + (jnp.log(nf / n_exact) / math.log(REL_MAX_DIST / n_exact)
                       * (REL_BUCKETS - n_exact)).astype(jnp.int32)
    return jnp.where(n < n_exact, n, jnp.minimum(large, REL_BUCKETS - 1))

def _head_bias(rel_bias, dist):
    q, t = dist.shape
    b = rel_bias[_rel_bucket(dist)].astype(jnp.float32)
    return b.reshape(q, t, NSA_KV_HEADS, NSA_GROUP).transpose(0, 2, 3, 1)

def _ada(c, w, b):
    mod = (jax.nn.silu(c) @ w + b)[:, None, :]
    return jnp.split(mod, ADA_CHUNKS, axis=-1)

def _sq_relu_mlp(h, w_in, w_out):
    return jnp.square(jax.nn.relu(h @ w_in)) @ w_out

def _nsa_project(h, w_in):
    b, t, _ = h.shape
    proj = h @ w_in
    o1 = NSA_Q_W
    o2 = o1 + 4 * NSA_KV_W
    o3 = o2 + 2 * NSA_KV_W
    qg = proj[..., :o1].reshape(b, t, NSA_KV_HEADS, NSA_GROUP, NSA_HEAD_DIM)
    kv_cs = proj[..., o1:o2].reshape(b, t, 4, NSA_KV_HEADS, NSA_HEAD_DIM)
    kv_win = proj[..., o2:o3].reshape(b, t, 2, NSA_KV_HEADS, NSA_HEAD_DIM)
    gates = jax.nn.sigmoid(proj[..., o3:].astype(jnp.float32)).reshape(b, t, 3, NSA_KV_HEADS, NSA_GROUP)
    return qg, kv_cs, kv_win, gates

def _nsa_compress(kv_pad, cmp_pos, w1, w2):
    b, tpad = kv_pad.shape[:2]
    n_chunks = tpad // CMP_STRIDE
    chunks = kv_pad[:, :, :2].reshape(b, n_chunks, CMP_STRIDE, 2, NSA_KV_HEADS, NSA_HEAD_DIM)
    w1 = w1.reshape(2, CMP_LEN, NSA_HEAD_DIM, CMP_HIDDEN)
    pos_bias = jnp.einsum('rld,rlde->re', cmp_pos, w1)
    pa = jnp.einsum('bnlrkd,rlde->bnrke', chunks, w1[:, :CMP_STRIDE])
    pb = jnp.einsum('bnlrkd,rlde->bnrke', chunks, w1[:, CMP_STRIDE:])
    hidden = jax.nn.gelu(pa[:, :-1] + pb[:, 1:] + pos_bias[:, None, :])
    out = jnp.einsum('bnrke,ref->bnrkf', hidden, w2)
    return out[:, :, 0], out[:, :, 1]

def _nsa_sparse_block(qg, q_pos, k_cmp, v_cmp, cmp_end, sel_kv, rel_bias):
    b, qc = qg.shape[:2]
    n_sel = sel_kv.shape[1]
    scale = NSA_HEAD_DIM ** -0.5
    dist_c = q_pos[:, None] - cmp_end[None, :]
    logits_c = jnp.einsum('bqkgd,bnkd->bqkgn', qg, k_cmp) * scale + _head_bias(rel_bias, dist_c)
    p_c = _masked_softmax(logits_c, (dist_c >= 0)[:, None, None, :])
    o_cmp = jnp.einsum('bqkgn,bnkd->bqkgd', p_c, v_cmp.astype(jnp.float32))
    imp = jnp.pad(p_c.sum(axis=3), ((0, 0), (0, 0), (0, 0), (1, 1)))
    imp = 0.5 * (imp[..., 1:] + imp[..., :-1])
    imp = imp.reshape(b, qc, NSA_KV_HEADS, n_sel, SEL_BLOCK // CMP_STRIDE).sum(-1)
    blk = jnp.arange(n_sel)[None, :]
    cur = (q_pos // SEL_BLOCK)[:, None]
    forced = (blk == 0) | (blk == cur) | (blk == cur - 1)
    valid = blk * SEL_BLOCK <= q_pos[:, None]
    score = jnp.where(forced[None, :, None, :], FORCE_SCORE, imp)
    score = jnp.where(valid[None, :, None, :], score, NEG_INF)
    n_cand = max(n_sel, SEL_TOP_N)
    score = jnp.pad(score, ((0, 0), (0, 0), (0, 0), (0, n_cand - n_sel)), constant_values=NEG_INF)
    top_val, top_idx = lax.top_k(score, SEL_TOP_N)
    sel_ok = top_val > 0.5 * NEG_INF
    top_idx = jnp.minimum(top_idx, n_sel - 1)
    bi = jnp.arange(b)[:, None, None, None]
    ki = jnp.arange(NSA_KV_HEADS)[None, None, :, None]
    kv_sel = sel_kv[bi, top_idx, :, :, ki]
    kpos = top_idx[..., None] * SEL_BLOCK + jnp.arange(SEL_BLOCK)
    dist_s = q_pos[None, :, None, None, None] - kpos
    mask_s = (sel_ok[..., None] & (dist_s >= 0)).reshape(b, qc, NSA_KV_HEADS, 1, SEL_TOP_N * SEL_BLOCK)
    table = rel_bias.reshape(REL_BUCKETS, NSA_KV_HEADS, NSA_GROUP).transpose(1, 0, 2)
    bias_s = table[jnp.arange(NSA_KV_HEADS)[None, None, :, None, None], _rel_bucket(dist_s)]
    bias_s = jnp.moveaxis(bias_s, -1, 3).reshape(b, qc, NSA_KV_HEADS, NSA_GROUP, SEL_TOP_N * SEL_BLOCK)
    logits_s = jnp.einsum('bqkgd,bqknsd->bqkgns', qg, kv_sel[..., 0, :])
    logits_s = logits_s.reshape(b, qc, NSA_KV_HEADS, NSA_GROUP, SEL_TOP_N * SEL_BLOCK) * scale + bias_s.astype(jnp.float32)
    p_s = _masked_softmax(logits_s, mask_s)
    v_sel = kv_sel[..., 1, :].reshape(b, qc, NSA_KV_HEADS, SEL_TOP_N * SEL_BLOCK, NSA_HEAD_DIM)
    o_sel = jnp.einsum('bqkgm,bqkmd->bqkgd', p_s, v_sel.astype(jnp.float32))
    return o_cmp, o_sel

def _nsa_sparse(qg, q_pos, kv_all, cmp_pos, w1, w2, rel_bias):
    b, t_kv = kv_all.shape[:2]
    t_pad = -(-t_kv // SEL_BLOCK) * SEL_BLOCK
    kv_pad = jnp.pad(kv_all, ((0, 0), (0, t_pad - t_kv), (0, 0), (0, 0), (0, 0)))
    k_cmp, v_cmp = _nsa_compress(kv_pad, cmp_pos, w1, w2)
    cmp_end = jnp.arange(k_cmp.shape[1]) * CMP_STRIDE + CMP_LEN - 1
    sel_kv = kv_pad[:, :, 2:].reshape(b, t_pad // SEL_BLOCK, SEL_BLOCK, 2, NSA_KV_HEADS, NSA_HEAD_DIM)
    tq = qg.shape[1]
    qb = SEL_Q_BLOCK if tq % SEL_Q_BLOCK == 0 else tq
    nq = tq // qb
    q_blocks = jnp.moveaxis(qg.reshape(b, nq, qb, NSA_KV_HEADS, NSA_GROUP, NSA_HEAD_DIM), 1, 0)
    pos_blocks = q_pos.reshape(nq, qb)
    o_cmp, o_sel = lax.map(
        lambda a: _nsa_sparse_block(a[0], a[1], k_cmp, v_cmp, cmp_end, sel_kv, rel_bias),
        (q_blocks, pos_blocks))
    shape = (b, tq, NSA_KV_HEADS, NSA_GROUP, NSA_HEAD_DIM)
    return jnp.moveaxis(o_cmp, 0, 1).reshape(shape), jnp.moveaxis(o_sel, 0, 1).reshape(shape)

def _window_attend(qg, q_pos, kv, k_pos, rel_bias):
    dist = q_pos[:, None] - k_pos[None, :]
    mask = (dist >= 0) & (dist <= WINDOW) & (k_pos >= 0)[None, :]
    logits = jnp.einsum('bqkgd,btkd->bqkgt', qg, kv[:, :, 0]) * NSA_HEAD_DIM ** -0.5 + _head_bias(rel_bias, dist)
    p = _masked_softmax(logits, mask[:, None, None, :])
    return jnp.einsum('bqkgt,btkd->bqkgd', p, kv[:, :, 1].astype(jnp.float32))

def _nsa_window_prompt(qg, kv_win, rel_bias):
    b, t = qg.shape[:2]
    nb = t // WIN_Q_BLOCK
    kv_pad = jnp.pad(kv_win, ((0, 0), (WINDOW, 0), (0, 0), (0, 0), (0, 0)))
    q_blocks = jnp.moveaxis(qg.reshape(b, nb, WIN_Q_BLOCK, NSA_KV_HEADS, NSA_GROUP, NSA_HEAD_DIM), 1, 0)

    def block(args):
        qblk, i = args
        start = i * WIN_Q_BLOCK
        kv = lax.dynamic_slice_in_dim(kv_pad, start, WINDOW + WIN_Q_BLOCK, axis=1)
        k_pos = start - WINDOW + jnp.arange(WINDOW + WIN_Q_BLOCK)
        q_pos = start + jnp.arange(WIN_Q_BLOCK)
        return _window_attend(qblk, q_pos, kv, k_pos, rel_bias)

    o = lax.map(block, (q_blocks, jnp.arange(nb)))
    return jnp.moveaxis(o, 0, 1).reshape(b, t, NSA_KV_HEADS, NSA_GROUP, NSA_HEAD_DIM)

def _nsa_output(o_cmp, o_sel, o_win, gates, w_out, dtype):
    b, t = gates.shape[:2]
    o = (gates[:, :, 0, ..., None] * o_cmp + gates[:, :, 1, ..., None] * o_sel
         + gates[:, :, 2, ..., None] * o_win)
    return o.reshape(b, t, NSA_Q_W).astype(dtype) @ w_out

def _nsa_prompt(h, w_in, cmp_pos, cmp_w1, cmp_w2, w_out, rel_bias):
    t = h.shape[1]
    qg, kv_cs, kv_win, gates = _nsa_project(h, w_in)
    o_cmp, o_sel = _nsa_sparse(qg, jnp.arange(t), kv_cs, cmp_pos, cmp_w1, cmp_w2, rel_bias)
    o_win = _nsa_window_prompt(qg, kv_win, rel_bias)
    out = _nsa_output(o_cmp, o_sel, o_win, gates, w_out, h.dtype)
    return out, kv_cs, kv_win[:, t - min(WINDOW, t):]

def _nsa_sample(h, kv_pages, win_buf, page_table, w_in, cmp_pos, cmp_w1, cmp_w2, w_out, rel_bias):
    b, t, _ = h.shape
    past_len = page_table.shape[1] * PAGE_SIZE
    qg, kv_cs, kv_win, gates = _nsa_project(h, w_in)
    past = kv_pages[page_table].reshape(b, past_len, 4, NSA_KV_HEADS, NSA_HEAD_DIM)
    kv_all = jnp.concatenate([past, kv_cs.astype(past.dtype)], axis=1)
    q_pos = past_len + jnp.arange(t)
    o_cmp, o_sel = _nsa_sparse(qg, q_pos, kv_all, cmp_pos, cmp_w1, cmp_w2, rel_bias)
    n_buf = win_buf.shape[1]
    kv_w_all = jnp.concatenate([win_buf, kv_win.astype(win_buf.dtype)], axis=1)
    k_pos = past_len - n_buf + jnp.arange(n_buf + t)
    o_win = _window_attend(qg, q_pos, kv_w_all, k_pos, rel_bias)
    out = _nsa_output(o_cmp, o_sel, o_win, gates, w_out, h.dtype)
    new_win = kv_w_all[:, kv_w_all.shape[1] - min(WINDOW, past_len + t):]
    return out, kv_cs, new_win

def _gla_scan(q, k, v, log_f, s0):
    b, t = q.shape[:2]
    c = HG_CHUNK if t % HG_CHUNK == 0 else t
    nc = t // c
    causal = np.tril(np.ones((c, c), dtype=bool))[None, :, :, None, None]

    def to_chunks(a):
        return jnp.moveaxis(a.astype(jnp.float32).reshape(b, nc, c, *a.shape[2:]), 1, 0)

    def step(s, inp):
        qc, kc, vc, gc = inp
        cum = jnp.cumsum(gc, axis=1)
        decay = jnp.exp(jnp.where(causal, cum[:, :, None] - cum[:, None, :], -jnp.inf))
        attn = jnp.einsum('bthk,btshk,bshk->bhts', qc, decay, kc)
        o = (jnp.einsum('bhts,bshv->bthv', attn, vc)
             + jnp.einsum('bthk,bhkv->bthv', qc * jnp.exp(cum), s))
        last = cum[:, -1]
        s_new = (jnp.exp(last)[..., None] * s
                 + jnp.einsum('bshk,bshv->bhkv', kc * jnp.exp(last[:, None] - cum), vc))
        return s_new, o

    s_final, o = lax.scan(step, s0.astype(jnp.float32),
                          (to_chunks(q), to_chunks(k), to_chunks(v), to_chunks(log_f)))
    return jnp.moveaxis(o, 0, 1).reshape(b, t, HG_HEADS, HG_DV), s_final

def _hgrn2(h, s0, lb, w_in, g_norm, w_out):
    b, t, _ = h.shape
    proj = h @ w_in
    wk = HG_HEADS * HG_DK
    wv = HG_HEADS * HG_DV
    q = jax.nn.silu(proj[..., :wk]).reshape(b, t, HG_HEADS, HG_DK)
    f = lb + (1.0 - lb) * jax.nn.sigmoid(proj[..., wk:2 * wk].astype(jnp.float32))
    v = proj[..., 2 * wk:2 * wk + wv].reshape(b, t, HG_HEADS, HG_DV)
    g = proj[..., 2 * wk + wv:].reshape(b, t, HG_HEADS, HG_DV)
    k = (1.0 - f).reshape(b, t, HG_HEADS, HG_DK)
    log_f = jnp.log(f).reshape(b, t, HG_HEADS, HG_DK)
    o, s_new = _gla_scan(q, k, v, log_f, s0)
    o = _rmsnorm(o, g_norm) * jax.nn.silu(g.astype(jnp.float32))
    return o.reshape(b, t, wv).astype(h.dtype) @ w_out, s_new.astype(h.dtype)

def _causal_conv(u, prev, w, bias):
    t = u.shape[1]
    full = jnp.concatenate([prev.astype(u.dtype), u], axis=1)
    y = sum(full[:, i:i + t] * w[i] for i in range(SSD_CONV_W)) + bias
    return y, full[:, t:]

def _ssd_scan(x, dt, a, bm, cm, s0):
    b, t = x.shape[:2]
    c = SSD_CHUNK if t % SSD_CHUNK == 0 else t
    nc = t // c
    causal = np.tril(np.ones((c, c), dtype=bool))[None, :, :, None, None]

    def to_chunks(arr):
        return jnp.moveaxis(arr.reshape(b, nc, c, *arr.shape[2:]), 1, 0)

    def step(s, inp):
        xc, dtc, bc, cc = inp
        cum = jnp.cumsum(dtc * a, axis=1)
        decay = jnp.exp(jnp.where(causal, cum[:, :, None] - cum[:, None, :], -jnp.inf))
        cb = jnp.einsum('btgn,bsgn->btsg', cc, bc)
        w = cb[..., None] * decay * dtc[:, None]
        y = (jnp.einsum('btsgh,bsghp->btghp', w, xc)
             + jnp.einsum('btgn,bghpn->btghp', cc, s) * jnp.exp(cum)[..., None])
        last = cum[:, -1]
        s_new = (jnp.exp(last)[..., None, None] * s
                 + jnp.einsum('bsgn,bsgh,bsghp->bghpn', bc, dtc * jnp.exp(last[:, None] - cum), xc))
        return s_new, y

    s_final, y = lax.scan(step, s0, (to_chunks(x), to_chunks(dt), to_chunks(bm), to_chunks(cm)))
    return jnp.moveaxis(y, 0, 1).reshape(b, t, SSD_GROUPS, SSD_HPG, SSD_HEAD_DIM), s_final

def _ssd(h, ssm0, conv0, w_in, conv_w, conv_b, dt_bias, a_log, d_skip, norm_w, w_out):
    b, t, _ = h.shape
    di = SSD_D_INNER
    gn = SSD_GROUPS * SSD_STATE
    proj = h @ w_in
    z = proj[..., :di]
    xbc, conv_new = _causal_conv(proj[..., di:di + SSD_CONV_DIM], conv0, conv_w, conv_b)
    xbc = jax.nn.silu(xbc.astype(jnp.float32))
    x = xbc[..., :di].reshape(b, t, SSD_GROUPS, SSD_HPG, SSD_HEAD_DIM)
    bm = xbc[..., di:di + gn].reshape(b, t, SSD_GROUPS, SSD_STATE)
    cm = xbc[..., di + gn:].reshape(b, t, SSD_GROUPS, SSD_STATE)
    dt = jax.nn.softplus(proj[..., di + SSD_CONV_DIM:].astype(jnp.float32) + dt_bias)
    dt = dt.reshape(b, t, SSD_GROUPS, SSD_HPG)
    a = -jnp.exp(a_log.astype(jnp.float32)).reshape(SSD_GROUPS, SSD_HPG)
    s0 = ssm0.astype(jnp.float32).reshape(b, SSD_GROUPS, SSD_HPG, SSD_HEAD_DIM, SSD_STATE)
    y, s_new = _ssd_scan(x, dt, a, bm, cm, s0)
    y = y + d_skip.astype(jnp.float32).reshape(SSD_GROUPS, SSD_HPG)[..., None] * x
    y = y.reshape(b, t, di) * jax.nn.silu(z.astype(jnp.float32))
    y = _rmsnorm(y.reshape(b, t, SSD_GROUPS, di // SSD_GROUPS), norm_w.reshape(SSD_GROUPS, di // SSD_GROUPS))
    out = y.reshape(b, t, di).astype(h.dtype) @ w_out
    return out, s_new.reshape(b, SSD_HEADS, SSD_HEAD_DIM, SSD_STATE).astype(h.dtype), conv_new

def setup_inputs(seed: int = 0) -> dict:
    key = jax.random.key(seed)
    keys = iter(jax.random.split(key, 48))
    f32 = jnp.float32

    def nrm(shape, scale):
        return jax.random.normal(next(keys), shape, f32) * scale

    n_pages = PAST_LEN // PAGE_SIZE
    n_phys = (DEC_BATCH * n_pages * 5) // 4
    n_buf = min(WINDOW, PAST_LEN)
    page_table = jax.random.permutation(next(keys), n_phys)[: DEC_BATCH * n_pages]
    page_table = page_table.reshape(DEC_BATCH, n_pages).astype(jnp.int32)
    dt0 = jnp.exp(jax.random.uniform(next(keys), (N_LAYERS_SSD, SSD_HEADS), f32,
                                     minval=math.log(1e-3), maxval=math.log(1e-1)))
    a0 = jax.random.uniform(next(keys), (N_LAYERS_SSD, SSD_HEADS), f32, minval=1.0, maxval=16.0)
    return {
        'x_prompt': nrm((BATCH, SEQ, D_MODEL), 1.0),
        'x_sample': nrm((DEC_BATCH, DEC_SEQ, D_MODEL), 1.0),
        'cache_nsa_kv': nrm((N_LAYERS_NSA, n_phys, PAGE_SIZE, 4, NSA_KV_HEADS, NSA_HEAD_DIM), 1.0),
        'cache_nsa_win': nrm((N_LAYERS_NSA, DEC_BATCH, n_buf, 2, NSA_KV_HEADS, NSA_HEAD_DIM), 1.0),
        'state_hgrn': nrm((N_LAYERS_HGRN, DEC_BATCH, HG_HEADS, HG_DK, HG_DV), 0.5),
        'state_ssd': nrm((N_LAYERS_SSD, DEC_BATCH, SSD_HEADS, SSD_HEAD_DIM, SSD_STATE), 0.1),
        'state_ssd_conv': nrm((N_LAYERS_SSD, DEC_BATCH, SSD_CONV_W - 1, SSD_CONV_DIM), 1.0),
        'page_table': page_table,
        'c_prompt': nrm((BATCH, D_MODEL), 1.0),
        'c_sample': nrm((DEC_BATCH, D_MODEL), 1.0),
        'rel_bias': nrm((REL_BUCKETS, NSA_HEADS), 0.5),
        'hgrn_lower_bounds': nrm((DEPTH, HG_HEADS * HG_DK), 0.5),
        'w_ada': nrm((DEPTH, D_MODEL, ADA_CHUNKS * D_MODEL), 0.5 * D_MODEL ** -0.5),
        'b_ada': nrm((DEPTH, ADA_CHUNKS * D_MODEL), 0.02),
        'norm_gains': 1.0 + nrm((DEPTH, 4, D_MODEL), 0.05),
        'w_mlp_in': nrm((DEPTH, D_MODEL, D_FF), D_MODEL ** -0.5),
        'w_mlp_out': nrm((DEPTH, D_FF, D_MODEL), D_FF ** -0.5),
        'nsa_w_in': nrm((N_LAYERS_NSA, D_MODEL, NSA_IN_W), D_MODEL ** -0.5),
        'nsa_cmp_pos': nrm((N_LAYERS_NSA, 2, CMP_LEN, NSA_HEAD_DIM), 0.1),
        'nsa_cmp_w1': nrm((N_LAYERS_NSA, 2, CMP_LEN * NSA_HEAD_DIM, CMP_HIDDEN), (CMP_LEN * NSA_HEAD_DIM) ** -0.5),
        'nsa_cmp_w2': nrm((N_LAYERS_NSA, 2, CMP_HIDDEN, NSA_HEAD_DIM), CMP_HIDDEN ** -0.5),
        'nsa_w_out': nrm((N_LAYERS_NSA, NSA_Q_W, D_MODEL), NSA_Q_W ** -0.5),
        'hg_w_in': nrm((N_LAYERS_HGRN, D_MODEL, HG_IN_W), D_MODEL ** -0.5),
        'hg_norm': 1.0 + nrm((N_LAYERS_HGRN, HG_DV), 0.05),
        'hg_w_out': nrm((N_LAYERS_HGRN, HG_HEADS * HG_DV, D_MODEL), (HG_HEADS * HG_DV) ** -0.5),
        'ssd_w_in': nrm((N_LAYERS_SSD, D_MODEL, SSD_IN_W), D_MODEL ** -0.5),
        'ssd_conv_w': nrm((N_LAYERS_SSD, SSD_CONV_W, SSD_CONV_DIM), SSD_CONV_W ** -0.5),
        'ssd_conv_b': nrm((N_LAYERS_SSD, SSD_CONV_DIM), 0.02),
        'ssd_dt_bias': dt0 + jnp.log(-jnp.expm1(-dt0)),
        'ssd_a_log': jnp.log(a0),
        'ssd_d': 1.0 + nrm((N_LAYERS_SSD, SSD_HEADS), 0.1),
        'ssd_norm': 1.0 + nrm((N_LAYERS_SSD, SSD_D_INNER), 0.05),
        'ssd_w_out': nrm((N_LAYERS_SSD, SSD_D_INNER, D_MODEL), SSD_D_INNER ** -0.5),
    }

def reference(x_prompt, x_sample, cache_nsa_kv, cache_nsa_win, state_hgrn, state_ssd, state_ssd_conv,
              page_table, c_prompt, c_sample, rel_bias, hgrn_lower_bounds, w_ada, b_ada, norm_gains,
              w_mlp_in, w_mlp_out, nsa_w_in, nsa_cmp_pos, nsa_cmp_w1, nsa_cmp_w2, nsa_w_out,
              hg_w_in, hg_norm, hg_w_out, ssd_w_in, ssd_conv_w, ssd_conv_b, ssd_dt_bias, ssd_a_log,
              ssd_d, ssd_norm, ssd_w_out):
    lb_p = jax.nn.softmax(hgrn_lower_bounds.astype(jnp.float32), axis=0)
    lower_bounds = jnp.cumsum(lb_p, axis=0) - lb_p[0]
    xp, xs = x_prompt, x_sample
    bp = xp.shape[0]
    kv_p, kv_s, win_p, win_s = [], [], [], []
    hg_p, hg_s, ssd_p, ssd_s, conv_p, conv_s = [], [], [], [], [], []
    for i in range(DEPTH):
        j = i // N_MIXERS
        kind = i % N_MIXERS
        shp_m, scp_m, gtp_m, shp_f, scp_f, gtp_f = _ada(c_prompt, w_ada[i], b_ada[i])
        shs_m, scs_m, gts_m, shs_f, scs_f, gts_f = _ada(c_sample, w_ada[i], b_ada[i])
        hp = _rmsnorm(xp, norm_gains[i, 0]) * (1.0 + scp_m) + shp_m
        hs = _rmsnorm(xs, norm_gains[i, 0]) * (1.0 + scs_m) + shs_m
        if kind == 0:
            mp, new_kv_p, new_win_p = _nsa_prompt(hp, nsa_w_in[j], nsa_cmp_pos[j], nsa_cmp_w1[j],
                                                  nsa_cmp_w2[j], nsa_w_out[j], rel_bias)
            ms, new_kv_s, new_win_s = _nsa_sample(hs, cache_nsa_kv[j], cache_nsa_win[j], page_table,
                                                  nsa_w_in[j], nsa_cmp_pos[j], nsa_cmp_w1[j],
                                                  nsa_cmp_w2[j], nsa_w_out[j], rel_bias)
            kv_p.append(new_kv_p)
            kv_s.append(new_kv_s)
            win_p.append(new_win_p)
            win_s.append(new_win_s)
        elif kind == 1:
            s0 = jnp.zeros((bp, HG_HEADS, HG_DK, HG_DV), jnp.float32)
            mp, new_hp = _hgrn2(hp, s0, lower_bounds[i], hg_w_in[j], hg_norm[j], hg_w_out[j])
            ms, new_hs = _hgrn2(hs, state_hgrn[j], lower_bounds[i], hg_w_in[j], hg_norm[j], hg_w_out[j])
            hg_p.append(new_hp)
            hg_s.append(new_hs)
        else:
            ssm0 = jnp.zeros((bp, SSD_HEADS, SSD_HEAD_DIM, SSD_STATE), jnp.float32)
            conv0 = jnp.zeros((bp, SSD_CONV_W - 1, SSD_CONV_DIM), xp.dtype)
            mp, new_sp, new_cp = _ssd(hp, ssm0, conv0, ssd_w_in[j], ssd_conv_w[j], ssd_conv_b[j],
                                      ssd_dt_bias[j], ssd_a_log[j], ssd_d[j], ssd_norm[j], ssd_w_out[j])
            ms, new_ss, new_cs = _ssd(hs, state_ssd[j], state_ssd_conv[j], ssd_w_in[j], ssd_conv_w[j],
                                      ssd_conv_b[j], ssd_dt_bias[j], ssd_a_log[j], ssd_d[j], ssd_norm[j],
                                      ssd_w_out[j])
            ssd_p.append(new_sp)
            ssd_s.append(new_ss)
            conv_p.append(new_cp)
            conv_s.append(new_cs)
        xp = xp + gtp_m * _rmsnorm(mp, norm_gains[i, 1])
        xs = xs + gts_m * _rmsnorm(ms, norm_gains[i, 1])
        hp = _rmsnorm(xp, norm_gains[i, 2]) * (1.0 + scp_f) + shp_f
        hs = _rmsnorm(xs, norm_gains[i, 2]) * (1.0 + scs_f) + shs_f
        xp = xp + gtp_f * _rmsnorm(_sq_relu_mlp(hp, w_mlp_in[i], w_mlp_out[i]), norm_gains[i, 3])
        xs = xs + gts_f * _rmsnorm(_sq_relu_mlp(hs, w_mlp_in[i], w_mlp_out[i]), norm_gains[i, 3])
    return (xp, xs, jnp.stack(kv_p), jnp.stack(kv_s), jnp.stack(win_p), jnp.stack(win_s),
            jnp.stack(hg_p), jnp.stack(hg_s), jnp.stack(ssd_p), jnp.stack(ssd_s),
            jnp.stack(conv_p), jnp.stack(conv_s))


_drawn_inputs = setup_inputs


def setup_inputs(seed=0):
    import zlib

    import numpy as np

    out = dict(_drawn_inputs(seed))
    spreads = {}
    factors = {}
    for name, (base, spread) in spreads.items():
        noise = np.random.default_rng([zlib.crc32(name.encode()), seed]).standard_normal(out[name].shape)
        drawn = base * np.exp(spread * noise) if base else spread * noise
        out[name] = jnp.asarray(drawn.astype(out[name].dtype))
    for name, factor in factors.items():
        out[name] = (out[name] * factor).astype(out[name].dtype)
    return out
```

```python
import math
from contextlib import ExitStack

import numpy as np
import concourse.bass as bass
from concourse import mybir

F32 = mybir.dt.float32
I32 = mybir.dt.int32
ALU = mybir.AluOpType
ACT = mybir.ActivationFunctionType
AX = mybir.AxisListType

D = 1024
DT = D // 128
SEQ = 256
NB = 8
T = SEQ + NB
DEPTH = 4
D_FF = 4 * D
FT = D_FF // 128
EPS = 1e-6
C = 1 + NB
NEG = -1e30

PAST = 1024
PAGE = 128
PAGES = PAST // PAGE
N_PHYS = NB * PAGES * 5 // 4
HEADS = 16
KV = 4
HD = 64
GRP = HEADS // KV
CMP = 16
N_CMP_P = SEQ // CMP - 1
N_CMP_S = PAST // CMP - 1
SEL = 64
WIN = 512
BUCKETS = 32

HG_H = 8
SSD_I = 2048
SSD_H = 32
SSD_P = 64
SSD_G = 8
SSD_N = 128
CONV = SSD_I + 2 * SSD_G * SSD_N
CT = CONV // 128
ZT = SSD_I // 128

SLOTS = 4
UC = 512
GELU_2C = 2.0 * math.sqrt(2.0 / math.pi)
LEVELS = (64, 32, 16, 8, 4, 2, 1)


def _bucket(dist):
    n = np.maximum(dist, 0)
    exact = BUCKETS // 2
    nf = np.maximum(n, 1).astype(np.float32)
    large = exact + (np.log(nf / np.float32(exact)) / np.float32(math.log(128 / exact))
                     * np.float32(BUCKETS - exact)).astype(np.int32)
    return np.where(n < exact, n, np.minimum(large, BUCKETS - 1))


def _onehot(dist):
    return (_bucket(np.asarray(dist))[None, :] == np.arange(BUCKETS)[:, None]).astype(np.float32)


def _constants():
    p = np.arange(128)
    wide, at = [], {}

    def put(name, a):
        a = np.asarray(a, np.float32).reshape(128, -1)
        at[name] = (sum(x.shape[1] for x in wide), a.shape[1])
        wide.append(a)

    put("ident", p[:, None] == p[None, :])
    put("flip", p[:, None] == 127 - p[None, :])
    s, t = p[:, None], p[None, :]
    put("levels", np.stack([(s // (2 * m) == t // (2 * m)) & (s % (2 * m) < m) & (t % (2 * m) >= m)
                            for m in LEVELS] + [s == t], 1))
    put("causal_add", np.where(t <= s, 0.0, NEG))
    put("causal_mul", np.concatenate([t >= s, np.ones((128, 128)), t >= s], 1))
    q = np.stack([p, p + 128], 1)
    seen = q[:, :, None] >= CMP * np.arange(N_CMP_P)[None, None, :] + 2 * CMP - 1
    put("cmp_mul", seen)
    put("cmp_add", np.where(seen, 0.0, NEG))
    put("block_no", np.broadcast_to(np.arange(1, 15), (128, 14)))
    r = np.arange(32)
    same = (r[:, None] // GRP == r[None, :] // GRP)
    put("group_sum", np.concatenate([same, np.zeros((96, 32))], 0))
    rows = np.zeros((128, 4, NB))
    for g in range(4):
        for i in range(32):
            rows[i, g, 2 * g + i // 16] = 1
    put("row_sample", rows)
    rows_t = np.zeros((128, 4, 32))
    for g in range(4):
        for i in range(32):
            rows_t[2 * g + i // 16, g, i] = 1
    put("sample_rows", rows_t)
    pick = np.zeros((128, HEADS))
    pick[np.arange(32), np.arange(32) % 16] = 1
    put("pick_head", pick)
    put("tok_row", (2.0 * p + 1)[:, None])
    put("chunk_row", 4.0 * CMP * (p % 8)[:, None] + 4.0 * np.arange(CMP)[None, :])
    wide = np.concatenate(wide, 1)

    narrow, bt = [], {}

    def put32(name, a):
        bt[name] = (sum(x.shape[1] for x in narrow), a.shape[1])
        narrow.append(a)

    put32("by_dist", _onehot(255 - np.arange(512)))
    put32("cmp_prompt", _onehot((np.arange(SEQ)[None, :]
                                 - (CMP * np.arange(N_CMP_P) + 2 * CMP - 1)[:, None]).reshape(-1)))
    put32("past", _onehot(PAST - np.arange(PAST)))
    put32("cmp_past", _onehot(PAST - (CMP * np.arange(64) + 2 * CMP - 1)))
    put32("here", _onehot(np.zeros(2, np.int64)))
    return wide, at, np.concatenate(narrow, 1), bt


WIDE, WIDE_AT, NARROW, NARROW_AT = _constants()


class Signal:

    def __init__(self, sem):
        self.sem, self.base, self.given = sem, 0, 0

    def at(self, k):
        return self.base + k

    def on(self, instruction, by=1, times=1):
        self.given += by * times
        return instruction.then_inc(self.sem, by)

    def close(self):
        self.base += self.given
        self.given = 0


def stepper(engine, counter):

    def step(instruction):
        counter.on(instruction)
        engine.wait_ge(counter.sem, counter.at(counter.given))

    return step


def bc(ap, axis, n):
    ap = ap.unsqueeze(axis)
    shape = list(ap.shape)
    shape[axis] = n
    return ap.broadcast_to(shape)


def hybrid_trunk(nc, a, outs, consts, stop=None):
    (y_p, y_s, kv_p, kv_s, win_p, win_s, hg_p, hg_s, ssd_p, ssd_s, conv_p, conv_s) = outs
    ctx = ExitStack()
    with ctx:
        def sb(name, shape, dt=F32):
            return ctx.enter_context(nc.sbuf_tensor(name, shape, dt))

        signals = []

        def signal(name):
            signals.append(Signal(ctx.enter_context(nc.semaphore(name))))
            return signals[-1]

        ring = sb("ring", [128, SLOTS, 8, UC])
        xT = sb("xT", [128, DT, T])
        hT = sb("hT", [128, DT, T])
        mT = sb("mT", [128, DT, T])
        mod = sb("mod", [128, 2, 6 * DT, C])
        coef = sb("coef", [128, DT, C])
        rstd = sb("rstd", [128, T])
        cT = sb("cT", [128, DT, 32])
        ada_tmp = sb("ada_tmp", [128, 128])
        wide = sb("wide", [128, WIDE.shape[1]])
        par = sb("par", [128, 593])
        ones = sb("ones", [128, 256])
        eps = sb("eps", [128, 1])
        col32 = sb("col32", [32, 4])
        lower = sb("lower", [128, DT])
        AW = 25328
        arena = sb("arena", [128, AW])
        PS = ctx.enter_context(nc.psum_tensor("PS", [128, 8, 512], F32))

        def con(name, rows=128):
            o, n = WIDE_AT[name]
            return wide[0:rows, o:o + n]

        ident = con("ident")

        class Place:

            def __init__(self, start=0):
                self.at = start

            def __call__(self, *shape, rows=128):
                n = int(np.prod(shape))
                v = arena[0:rows, self.at:self.at + n]
                self.at += n
                assert self.at <= AW, self.at
                if len(shape) == 2:
                    v = v.rearrange("p (a b) -> p a b", a=shape[0])
                elif len(shape) == 3:
                    v = v.rearrange("p (a b c) -> p a b c", a=shape[0], b=shape[1])
                elif len(shape) == 4:
                    v = v.rearrange("p (a b c d) -> p a b c d", a=shape[0], b=shape[1], c=shape[2])
                return v

        gain = lambda l, n: par[:, (4 * l + n) * DT:(4 * l + n + 1) * DT]
        b_ada = lambda l, m, n: par[:, 128 + l * 48 + m:128 + l * 48 + m + n]
        conv_w = par[:, 320:448].rearrange("p (i t) -> p i t", i=4)
        conv_b = par[:, 448:480]
        lbs = par[:, 480:512].rearrange("p (l t) -> p l t", l=DEPTH)
        ssd_gain = par[:, 512:528]
        hg_gain = par[:, 528:529]
        cmp_pos = par[:, 529:593].rearrange("p (l r j) -> p l r j", l=2, r=2)

        dist_dram = nc.dram_tensor("bias_by_distance", (HEADS, 512), F32, kind="Internal").ap()
        bias_dram = nc.dram_tensor("bias_matrices", (128, 2 * HEADS * 128 + 2 * HEADS * N_CMP_P), F32,
                                   kind="Internal").ap()

        w_loaded = [signal(f"w_loaded{s}") for s in range(SLOTS)]
        w_used = signal("w_used")
        loaded = signal("loaded")
        loaded2 = signal("loaded2")
        stored = signal("stored")
        stored2 = signal("stored2")
        mm_ready = signal("mm_ready")
        mm_taken = signal("mm_taken")
        aux_ready = signal("aux_ready")
        aux_taken = signal("aux_taken")
        pv_ready = signal("pv_ready")
        dve_step = signal("dve_step")
        act_step = signal("act_step")
        pool_step = signal("pool_step")
        given = signal("given")
        taken = signal("taken")
        fetched = [signal(f"fetched{i}") for i in range(4)]
        ada_loaded = [signal(f"ada_loaded{j}") for j in range(3)]
        ada_ready = signal("ada_ready")
        ada_moved = signal("ada_moved")
        ada_turned = signal("ada_turned")
        ada_added = signal("ada_added")

        def end_stage():
            for s in signals:
                s.close()

        def cols_of(w, k0=0):
            v = w[k0 * 128:(k0 + 8) * 128, :].rearrange("(k p) n -> p k n", p=128)
            return lambda k, i: v[:, :, bass.ds((k + 4 * i) * UC, UC)]

        def mlp_out_unit(w):
            v = w.rearrange("(g k p) n -> g p k n", g=4, p=128)
            return lambda k, i: v[k % 4, :, :, bass.ds((k // 4 + i) * UC, UC)]

        def ssd_out_unit(w):
            v = w.rearrange("(g k p) n -> g p k n", g=2, p=128)
            return lambda k, i: v[k % 2, :, :, (k // 2) * UC:(k // 2 + 1) * UC]

        units = []

        def group(n, source, loops=False):
            units.extend((source, k, loops) for k in range(n))

        group(12, cols_of(a["w_ada"][0]), True)
        for l in range(DEPTH):
            if l % 3 == 0:
                group(5, cols_of(a["nsa_w_in"][l // 3]))
                group(2, cols_of(a["nsa_w_out"][l // 3]))
            elif l % 3 == 1:
                group(8, cols_of(a["hg_w_in"][0]))
                group(2, cols_of(a["hg_w_out"][0]))
            else:
                group(12, cols_of(a["ssd_w_in"][0]))
                group(4, ssd_out_unit(a["ssd_w_out"][0]))
            group(8, cols_of(a["w_mlp_in"][l]), True)
            group(8, mlp_out_unit(a["w_mlp_out"][l]), True)
        st = {"issued": 0, "used": 0}

        def issue(sp, upto):
            upto = min(upto, len(units))
            while st["issued"] < upto:
                u = st["issued"]
                source, k, loops = units[u]
                n = 0
                while loops and u + 4 * (n + 1) <= upto and units[u + 4 * n + 3][0] is source:
                    n += 1
                if n >= 2 and u >= SLOTS:
                    with sp.Fori(0, n) as i:
                        for j in range(4):
                            sp.wait_ge(w_used.sem, u + j - SLOTS + 1 + 4 * i)
                            w_loaded[(u + j) % SLOTS].on(
                                sp.dma_start(ring[:, (u + j) % SLOTS, :, :], source(k + j, i)), 16, n)
                    st["issued"] += 4 * n
                else:
                    if u >= SLOTS:
                        sp.wait_ge(w_used.sem, u - SLOTS + 1)
                    w_loaded[u % SLOTS].on(sp.dma_start(ring[:, u % SLOTS, :, :], source(k, 0)), 16)
                    st["issued"] += 1

        def stream(sp, n):
            issue(sp, st["used"] + n + SLOTS)

        def unit(pe, u, i=0):
            pe.wait_ge(w_loaded[u % SLOTS].sem, 16 * (u // SLOTS + 1) + 16 * i)
            return ring[:, u % SLOTS, :, :]

        def stage_prepare():
            P = Place()
            xtok = P(3, D)
            ctok = P(D, rows=C)
            rows = P(6, 128)
            nar = arena[0:32, P.at:P.at + NARROW.shape[1]]
            P.at += NARROW.shape[1]
            relb = P(HEADS, rows=32)
            bd = P(512, rows=HEADS)
            skew = P(2, HEADS, 128)
            mats = P(2, HEADS, 128)
            bcmp = P(2, HEADS, N_CMP_P)
            lbe = P(DEPTH, DT)
            lbt = P(2, DT)
            tables = [(a["norm_gains"].rearrange("l n (t p) -> (l n t) p", p=128), 0, 0, 128),
                      (a["b_ada"].rearrange("l (t p) -> (l t) p", p=128)[0:96], 1, 0, 96),
                      (a["b_ada"].rearrange("l (t p) -> (l t) p", p=128)[96:192], 2, 0, 96),
                      (a["ssd_conv_w"][0].rearrange("i (t p) -> (i t) p", p=128), 3, 0, 128),
                      (a["ssd_conv_b"][0].rearrange("(t p) -> t p", p=128), 4, 0, 32),
                      (a["hgrn_lower_bounds"].rearrange("l (t p) -> (l t) p", p=128), 4, 32, 32),
                      (a["ssd_norm"][0].rearrange("(t p) -> t p", p=128), 4, 64, 16),
                      (a["hg_norm"], 4, 80, 1),
                      (a["nsa_cmp_pos"].rearrange("l r (j m) d -> (l r j) (m d)", m=2), 5, 0, 64)]
            spans = [(0, 128, 0), (1, 96, 128), (2, 96, 224), (3, 128, 320), (4, 81, 448), (5, 64, 529)]
            n_loads = 12 + len(tables)

            with nc.Block() as block:
                @block.sync
                def _(sp):
                    for dst, src in [(wide[:, :], consts[0]), (nar, consts[1]),
                                     (xtok[:, 0:2, :], a["x_prompt"][0].rearrange("(i p) n -> p i n", p=128)),
                                     (xtok[0:NB, 2, :], a["x_sample"][:, 0, :]),
                                     (ctok[0:1, :], a["c_prompt"]), (ctok[1:C, :], a["c_sample"]),
                                     (relb, a["rel_bias"])]:
                        loaded.on(sp.dma_start(dst, src), 16)
                    for src, i, r, n in tables:
                        loaded.on(sp.dma_start(rows[r:r + n, i, :], src), 16)
                    for j, name in enumerate(("ssd_dt_bias", "ssd_a_log", "ssd_d")):
                        loaded.on(sp.dma_start(col32[:, j:j + 1], a[name].rearrange("o h -> h o")), 16)
                    issue(sp, SLOTS)
                    sp.wait_ge(given.sem, given.at(1))
                    loaded2.on(sp.dma_start(dist_dram, bd), 16)
                    sp.wait_ge(loaded2.sem, loaded2.at(16))
                    for h in range(2):
                        src = bass.AP(dist_dram.tensor, 128 - 128 * h, [[1, 128], [512, HEADS], [1, 128]])
                        loaded2.on(sp.dma_start(skew[:, h], src), 16)
                    sp.wait_ge(given.sem, given.at(2))
                    nb = 2 * HEADS * 128
                    stored.on(sp.dma_start(bias_dram[:, 0:nb], mats.rearrange("p a b c -> p (a b c)")), 16)
                    stored.on(sp.dma_start(bias_dram[:, nb:], bcmp.rearrange("p a b c -> p (a b c)")), 16)
                    sp.wait_ge(stored.sem, stored.at(32))

                @block.vector
                def _(v):
                    step = stepper(v, dve_step)
                    nc.vector.memset(eps[:, :], EPS)
                    nc.vector.memset(cT[:, :, :], 0.0)
                    step(nc.vector.memset(ones[:, :], 1.0))
                    for n, (i, r, o) in enumerate(spans):
                        v.wait_ge(mm_ready.sem, mm_ready.at(n + 1))
                        mm_taken.on(nc.vector.tensor_copy(par[:, o:o + r], PS[:, n % 4, 0:r]))
                    v.wait_ge(mm_ready.sem, mm_ready.at(7))
                    mm_taken.on(nc.vector.tensor_copy(mT[:, :, 0:C],
                                                      PS[:, 2, 0:DT * C].rearrange("p (t c) -> p t c", c=C)))
                    for n in range(DT):
                        v.wait_ge(mm_ready.sem, mm_ready.at(8 + n))
                        mm_taken.on(nc.vector.tensor_copy(xT[:, n, :], PS[:, (7 + n) % 4, 0:T]))
                    v.wait_ge(aux_ready.sem, aux_ready.at(1))
                    given.on(nc.vector.tensor_copy(bd, PS[0:HEADS, 4, :]))
                    v.wait_ge(aux_ready.sem, aux_ready.at(2))
                    cadd = con("cmp_add").rearrange("p (i n) -> p i n", i=2)
                    for i in range(2):
                        src = PS[:, 5, i * 240:(i + 1) * 240].rearrange("p (n h) -> p h n", h=HEADS)
                        step(nc.vector.tensor_tensor(bcmp[:, i], src, bc(cadd[:, i], 1, HEADS), ALU.add))
                    for n in range(8):
                        v.wait_ge(aux_ready.sem, aux_ready.at(3 + n))
                        src = PS[:, 4 + n % 4, :].rearrange("p (h t) -> p h t", h=4)
                        dst = mats[:, n // 4, 4 * (n % 4):4 * (n % 4) + 4, :]
                        if n < 4:
                            ins = nc.vector.tensor_tensor(dst, src, bc(con("causal_add"), 1, 4), ALU.add)
                        else:
                            ins = nc.vector.tensor_copy(dst, src)
                        step(ins)
                        v.sem_inc(aux_taken.sem, 1)
                        aux_taken.given += 1
                    v.sem_inc(given.sem, 1)
                    given.given += 1
                    step(nc.vector.tensor_tensor(lbt[:, 0], lbs[:, 0], lbs[:, 1], ALU.max))
                    for l in range(2, DEPTH):
                        step(nc.vector.tensor_tensor(lbt[:, 0], lbt[:, 0], lbs[:, l], ALU.max))
                    step(nc.vector.tensor_tensor(lbe, lbs, bc(lbt[:, 0], 1, DEPTH), ALU.subtract))
                    v.sem_inc(taken.sem, 1)
                    taken.given += 1
                    v.wait_ge(act_step.sem, act_step.at(2))
                    step(nc.vector.tensor_tensor(lbt[:, 0], lbe[:, 0], lbe[:, 1], ALU.add))
                    for l in range(2, DEPTH):
                        step(nc.vector.tensor_tensor(lbt[:, 0], lbt[:, 0], lbe[:, l], ALU.add))
                    step(nc.vector.reciprocal(lbt[:, 1], lbt[:, 0]))
                    step(nc.vector.tensor_tensor(lbe, lbe, bc(lbt[:, 1], 1, DEPTH), ALU.mult))
                    step(nc.vector.tensor_tensor(lower[:, :], lbe[:, 0], lbe[:, 1], ALU.add))
                    step(nc.vector.tensor_tensor(lower[:, :], lower[:, :], lbe[:, 0], ALU.subtract))
                    v.wait_ge(act_step.sem, act_step.at(3))
                    step(nc.vector.tensor_scalar_mul(col32[:, 1:2], col32[:, 1:2], -1.0))

                @block.scalar
                def _(act):
                    step = stepper(act, act_step)
                    act.wait_ge(mm_taken.sem, mm_taken.at(7))
                    step(nc.scalar.activation(cT[:, :, 0:C], mT[:, :, 0:C], ACT.Silu))
                    act.wait_ge(taken.sem, taken.at(1))
                    step(nc.scalar.activation(lbe, lbe, ACT.Exp))
                    step(nc.scalar.activation(col32[:, 1:2], col32[:, 1:2], ACT.Exp))

                @block.tensor
                def _(pe):
                    pe.wait_ge(loaded.sem, loaded.at(16 * 19))
                    for n, (i, r, o) in enumerate(spans):
                        if n >= 4:
                            pe.wait_ge(mm_taken.sem, mm_taken.at(n - 3))
                        mm_ready.on(nc.tensor.transpose(PS[:, n % 4, 0:r], rows[0:r, i, :], ident[0:r, 0:r]))
                    pe.wait_ge(mm_taken.sem, mm_taken.at(3))
                    for t in range(DT):
                        ins = nc.tensor.transpose(PS[:, 2, t * C:(t + 1) * C], ctok[:, t * 128:(t + 1) * 128],
                                                  ident[0:C, 0:C])
                    mm_ready.on(ins)
                    for t in range(DT):
                        pe.wait_ge(mm_taken.sem, mm_taken.at(t + 4))
                        b = (7 + t) % 4
                        for i in range(2):
                            nc.tensor.transpose(PS[:, b, i * 128:(i + 1) * 128],
                                                xtok[:, i, t * 128:(t + 1) * 128], ident)
                        mm_ready.on(nc.tensor.transpose(PS[:, b, SEQ:T], xtok[0:NB, 2, t * 128:(t + 1) * 128],
                                                        ident[0:NB, 0:NB]))
                    o, n = NARROW_AT["by_dist"]
                    aux_ready.on(nc.tensor.matmul(PS[0:HEADS, 4, :], relb, nar[:, o:o + n], start=True, stop=True))
                    o, _n = NARROW_AT["cmp_prompt"]
                    for i in range(2):
                        for n in range(N_CMP_P):
                            w = nar[:, o + n * SEQ + i * 128:o + n * SEQ + (i + 1) * 128]
                            ins = nc.tensor.matmul(PS[:, 5, i * 240 + n * HEADS:i * 240 + (n + 1) * HEADS],
                                                   w, relb, start=True, stop=True)
                    aux_ready.on(ins)
                    pe.wait_ge(loaded2.sem, loaded2.at(48))
                    pe.wait_ge(given.sem, given.at(1))
                    pe.wait_ge(dve_step.sem, dve_step.at(3))
                    for n in range(8):
                        if n >= 4:
                            pe.wait_ge(aux_taken.sem, aux_taken.at(n - 3))
                        aux_ready.on(nc.tensor.matmul(
                            PS[:, 4 + n % 4, :], con("flip"),
                            skew[:, n // 4, 4 * (n % 4):4 * (n % 4) + 4, :].rearrange("p h t -> p (h t)"),
                            start=True, stop=True))
            end_stage()

        def ada_product(pe, w, bank):
            for k in range(8):
                for m in range(4):
                    ins = nc.tensor.matmul(PS[32 * m:32 * m + 32, bank, 0:128], cT[:, k, :],
                                           w[:, k, m * 128:(m + 1) * 128], start=k == 0, stop=k == 7)
            return ins

        def ada_bias(l, bank, i, first, turn):
            dst = mod[:, l % 2, bass.ds(i * turn + first, 4), :]
            bias = par[:, bass.ds(i * turn + (128 + l * 48 + first), 4)]
            src = PS[:, bank, 0:128].rearrange("p (m c) -> p m c", c=32)[:, :, 0:C]
            return nc.vector.tensor_tensor(dst, src, bc(bias, 2, C), ALU.add)

        def stage_ada(l):
            n0 = st["used"]
            with nc.Block() as block:
                @block.sync
                def _(sp):
                    stream(sp, 12)

                @block.tensor
                def _(pe):
                    with pe.Fori(0, 3) as i:
                        for j in range(4):
                            w = unit(pe, n0 + j, i)
                            w_used.on(ada_product(pe, w, 0), 1, 3)
                            pe.wait_ge(ada_moved.sem, ada_moved.at(j + 1) + 4 * i)
                            ada_turned.on(nc.tensor.transpose(PS[:, 1, 0:128], ada_tmp[:, :], ident), 1, 3)

                @block.vector
                def _(v):
                    with v.Fori(0, 3) as i:
                        for j in range(4):
                            v.wait_ge(w_used.sem, n0 + j + 1 + 4 * i)
                            ada_moved.on(nc.vector.tensor_copy(ada_tmp[:, :], PS[:, 0, 0:128]), 1, 3)
                            v.wait_ge(ada_turned.sem, ada_turned.at(j + 1) + 4 * i)
                            ada_added.on(ada_bias(l, 1, i, 4 * j, 16), 1, 3)
            st["used"] += 12
            end_stage()

        def stage_norm(l, which):
            post = which % 2
            src = mT if post else xT
            part = 3 * (which // 2)
            md = mod[:, l % 2]
            with nc.Block() as block:
                @block.scalar
                def _(act):
                    for t in range(DT):
                        given.on(nc.scalar.activation(hT[:, t, :], src[:, t, :], ACT.Square))
                    step = stepper(act, act_step)
                    act.wait_ge(mm_ready.sem, mm_ready.at(1))
                    step(nc.scalar.activation(rstd[:, :], PS[:, 0, 0:T], ACT.Ln, bias=eps[:, :], scale=1.0 / D))
                    step(nc.scalar.activation(rstd[:, :], rstd[:, :], ACT.Exp, scale=-0.5))
                    if not post:
                        for t in range(DT):
                            act.wait_ge(taken.sem, taken.at(t + 1))
                            nc.scalar.activation(hT[:, t, 0:SEQ], hT[:, t, 0:SEQ], ACT.Identity,
                                                 bias=md[:, part * DT + t, 0:1])

                @block.tensor
                def _(pe):
                    for t in range(DT):
                        pe.wait_ge(given.sem, given.at(t + 1))
                        ins = nc.tensor.matmul(PS[:, 0, 0:T], ones[:, 0:128], hT[:, t, :], start=t == 0,
                                               stop=t == DT - 1)
                    mm_ready.on(ins)

                @block.vector
                def _(v):
                    step = stepper(v, dve_step)
                    g = bc(gain(l, which), 2, C)
                    if post:
                        step(nc.vector.tensor_tensor(coef[:, :, :], md[:, (part + 2) * DT:(part + 3) * DT, :], g,
                                                     ALU.mult))
                    else:
                        step(nc.vector.tensor_scalar_add(coef[:, :, :], md[:, (part + 1) * DT:(part + 2) * DT, :],
                                                         1.0))
                        step(nc.vector.tensor_tensor(coef[:, :, :], coef[:, :, :], g, ALU.mult))
                    v.wait_ge(act_step.sem, act_step.at(2))
                    tail = bc(rstd[:, SEQ:T], 1, DT)
                    if post:
                        step(nc.vector.tensor_tensor(mT[:, :, SEQ:T], mT[:, :, SEQ:T], tail, ALU.mult))
                        step(nc.vector.tensor_tensor(mT[:, :, SEQ:T], mT[:, :, SEQ:T], coef[:, :, 1:C], ALU.mult))
                        step(nc.vector.tensor_tensor(xT[:, :, SEQ:T], xT[:, :, SEQ:T], mT[:, :, SEQ:T], ALU.add))
                        for t in range(DT):
                            step(nc.vector.scalar_tensor_tensor(hT[:, t, 0:SEQ], mT[:, t, 0:SEQ], coef[:, t, 0:1],
                                                                rstd[:, 0:SEQ], ALU.mult, ALU.mult))
                            nc.vector.tensor_tensor(xT[:, t, 0:SEQ], xT[:, t, 0:SEQ], hT[:, t, 0:SEQ], ALU.add)
                    else:
                        for t in range(DT):
                            taken.on(nc.vector.scalar_tensor_tensor(hT[:, t, 0:SEQ], xT[:, t, 0:SEQ],
                                                                    coef[:, t, 0:1], rstd[:, 0:SEQ],
                                                                    ALU.mult, ALU.mult))
                        s = hT[:, :, SEQ:T]
                        step(nc.vector.tensor_tensor(s, xT[:, :, SEQ:T], tail, ALU.mult))
                        step(nc.vector.tensor_tensor(s, s, coef[:, :, 1:C], ALU.mult))
                        step(nc.vector.tensor_tensor(s, s, md[:, part * DT:(part + 1) * DT, 1:C], ALU.add))
            end_stage()

        def stage_mlp(l):
            P = Place()
            u = P(FT, T)
            aw = P(3, 8, UC)
            n0 = st["used"]
            more = l + 1 < DEPTH
            if more:
                ada_v = a["w_ada"][l + 1].rearrange("(k p) n -> p k n", p=128)

            def ada_load(sp, j, it, i=None):
                if it or i is not None:
                    sp.wait_ge(ada_ready.sem, ada_ready.at(3 * (it - 1) + j + 1) + (0 if i is None else 3 * i))
                c = (3 * it + j) * UC
                src = ada_v[:, :, c:c + UC] if i is None else ada_v[:, :, bass.ds(c + 3 * UC * i, UC)]
                ada_loaded[j].on(sp.dma_start(aw[:, j], src), 16, 1 if i is None else 2)

            with nc.Block() as block:
                @block.sync
                def _(sp):
                    for it in (0, 1, 3):
                        if it == 1:
                            assert st["issued"] == n0 + 8
                            source, k, _loops = units[n0 + 8]
                            with sp.Fori(0, 2) as i:
                                for j in range(4):
                                    if j < 3 and more:
                                        ada_load(sp, j, 1, i)
                                    s = (n0 + 8 + j) % SLOTS
                                    sp.wait_ge(w_used.sem, n0 + 8 + j - SLOTS + 1 + 4 * i)
                                    w_loaded[s].on(sp.dma_start(ring[:, s, :, :], source(j, i)), 16, 2)
                            st["issued"] += 8
                        else:
                            for j in range(4):
                                if j < 3 and more:
                                    ada_load(sp, j, it)
                                issue(sp, n0 + 4 * it + 4 + j + 1)

                def ada_turn(pe, j, it, i, banks):
                    if j >= 0:
                        pe.wait_ge(ada_moved.sem, ada_moved.at(3 * it + j + 1) + 3 * i)
                        if it or j:
                            pe.wait_ge(ada_added.sem, ada_added.at(3 * it + j) + 3 * i)
                        ada_turned.on(nc.tensor.transpose(PS[:, banks + 1, 0:128], ada_tmp[:, :], ident), 1, 2)
                    if j < 2:
                        pe.wait_ge(ada_loaded[j + 1].sem, ada_loaded[j + 1].at(16 * (it + 1)) + 16 * i)
                        ada_ready.on(ada_product(pe, aw[:, j + 1], banks), 1, 2)

                @block.tensor
                def _(pe):
                    with pe.Fori(0, 2) as i:
                        for j in range(4):
                            w = unit(pe, n0 + j, i)
                            for m in range(4):
                                pe.wait_ge(mm_taken.sem, mm_taken.at(4 * j + m - 3) + 16 * i)
                                for k in range(8):
                                    ins = nc.tensor.matmul(PS[:, m, 0:T], w[:, k, m * 128:(m + 1) * 128],
                                                           hT[:, k, :], start=k == 0, stop=k == 7)
                                (mm_ready if m < 3 else w_used).on(ins, 1, 2)
                            if more:
                                ada_turn(pe, j - 1, 0, i, 4)
                    pe.wait_ge(given.sem, given.at(32))
                    if more:
                        pe.wait_ge(ada_added.sem, ada_added.at(6))
                    with pe.Fori(0, 2) as i:
                        pe.wait_ge(aux_taken.sem, aux_taken.at(0) + 4 * i)
                        for j in range(4):
                            w = unit(pe, n0 + 8 + j, i)
                            for m in range(4):
                                for k in range(8):
                                    ins = nc.tensor.matmul(PS[:, 4 + m, 0:T], w[:, k, m * 128:(m + 1) * 128],
                                                           u[:, 8 * j + k, :], start=j == 0 and k == 0,
                                                           stop=j == 3 and k == 7)
                            w_used.on(ins, 1, 2)
                            if more:
                                ada_turn(pe, j - 1, 2, i, 0)

                @block.scalar
                def _(act):
                    with act.Fori(0, 2) as i:
                        for j in range(4):
                            for m in range(4):
                                if m < 3:
                                    act.wait_ge(mm_ready.sem, mm_ready.at(3 * j + m + 1) + 12 * i)
                                else:
                                    act.wait_ge(w_used.sem, n0 + j + 1 + 4 * i)
                                mm_taken.on(nc.scalar.activation(
                                    u[:, bass.ds(i * 16 + 4 * j + m, 1), :].rearrange("p a n -> p (a n)"),
                                    PS[:, m, 0:T], ACT.Relu), 1, 2)
                    with act.Fori(0, 2) as i:
                        act.wait_ge(w_used.sem, n0 + 12 + 4 * i)
                        for m in range(4):
                            aux_taken.on(nc.scalar.activation(
                                mT[:, bass.ds(i * 4 + m, 1), :].rearrange("p a n -> p (a n)"),
                                PS[:, 4 + m, 0:T], ACT.Copy), 1, 2)

                @block.vector
                def _(v):
                    def ada_turn(j, it, i, banks):
                        if j >= 0:
                            v.wait_ge(ada_turned.sem, ada_turned.at(3 * it + j + 1) + 3 * i)
                            ada_added.on(ada_bias(l + 1, banks + 1, i, 12 * it + 4 * j, 12), 1, 2)
                        if j < 2:
                            v.wait_ge(ada_ready.sem, ada_ready.at(3 * it + j + 2) + 3 * i)
                            ada_moved.on(nc.vector.tensor_copy(ada_tmp[:, :], PS[:, banks, 0:128]), 1, 2)

                    with v.Fori(0, 2) as i:
                        for j in range(4):
                            for m in range(4):
                                v.wait_ge(mm_taken.sem, mm_taken.at(4 * j + m + 1) + 16 * i)
                                w = u[:, bass.ds(i * 16 + 4 * j + m, 1), :].rearrange("p a n -> p (a n)")
                                given.on(nc.vector.tensor_tensor(w, w, w, ALU.mult), 1, 2)
                            if more:
                                ada_turn(j - 1, 0, i, 4)
                    if more:
                        with v.Fori(0, 2) as i:
                            for j in range(4):
                                ada_turn(j - 1, 2, i, 0)
            st["used"] += 16
            end_stage()

        def stage_output():
            ytok = Place()(3, D)
            with nc.Block() as block:
                @block.tensor
                def _(pe):
                    for i in range(3):
                        n = 128 if i < 2 else NB
                        for h in range(2):
                            if i:
                                pe.wait_ge(mm_taken.sem, mm_taken.at(2 * i + h - 1))
                            for t in range(4):
                                ins = nc.tensor.transpose(PS[0:n, h, t * 128:(t + 1) * 128],
                                                          xT[:, 4 * h + t, i * 128:i * 128 + n], ident)
                            mm_ready.on(ins)

                @block.vector
                def _(v):
                    for i in range(3):
                        n = 128 if i < 2 else NB
                        for h in range(2):
                            v.wait_ge(mm_ready.sem, mm_ready.at(2 * i + h + 1))
                            mm_taken.on(nc.vector.tensor_copy(ytok[0:n, i, h * 512:(h + 1) * 512],
                                                              PS[0:n, h, :]))

                @block.sync
                def _(sp):
                    sp.wait_ge(mm_taken.sem, mm_taken.at(6))
                    stored.on(sp.dma_start(y_p[0].rearrange("(i p) n -> p i n", p=128), ytok[:, 0:2, :]), 16)
                    stored.on(sp.dma_start(y_s[:, 0, :], ytok[0:NB, 2, :]), 16)
                    sp.wait_ge(stored.sem, stored.at(32))
            end_stage()

        scores_ready = signal("scores_ready")
        scores_taken = signal("scores_taken")
        max_ready = signal("max_ready")
        exp_ready = signal("exp_ready")
        probs_ready = signal("probs_ready")
        pt_ready = signal("pt_ready")
        pt_taken = signal("pt_taken")
        pt_taken2 = signal("pt_taken2")
        out_ready = signal("out_ready")
        out_taken = signal("out_taken")
        imp_ready = signal("imp_ready")
        row_base = sb("row_base", [128, 256])
        row_no = sb("row_no", [128, 256], I32)
        page_no = sb("page_no", [128, 68], I32)
        cmp_rows = row_no[:, 0:128].rearrange("p (r g l) -> p r g l", r=2, g=4)
        tok_rows = row_no[:, 128:256].rearrange("p (r b) -> p r b", r=2)
        cache_rows = a["cache_nsa_kv"].rearrange("l g t r k d -> (l g t r) (k d)")

        def planned(per_unit, n0):
            plan, n = [], 0
            for u, m in enumerate(per_unit):
                for j in range(m):
                    if j == m - 1:
                        plan.append((w_used, n0 + u + 1))
                    else:
                        n += 1
                        plan.append((mm_ready, mm_ready.at(n)))
            return plan

        def stage_rows():
            with nc.Block() as block:
                @block.sync
                def _(sp):
                    pt = a["page_table"]
                    for g in range(4):
                        src = bass.AP(pt.tensor, g * 16, [[1, 16], [0, 8], [1, 1]])
                        loaded.on(sp.dma_start(page_no[:, g:g + 1], src), 16)
                    loaded.on(sp.dma_start(page_no[:, 4:68], bass.AP(pt.tensor, 0, [[0, 128], [1, 64]])), 16)

                @block.vector
                def _(v):
                    step = stepper(v, dve_step)
                    v.wait_ge(loaded.sem, loaded.at(80))
                    pf = Place()(68)
                    step(nc.vector.tensor_copy(pf, page_no[:, :]))
                    step(nc.vector.tensor_scalar_mul(pf, pf, 4.0 * PAGE))
                    cr = row_base[:, 0:128].rearrange("p (r g l) -> p r g l", r=2, g=4)
                    for g in range(4):
                        step(nc.vector.tensor_scalar_add(cr[:, 0, g], con("chunk_row"), pf[:, g:g + 1]))
                    step(nc.vector.tensor_scalar_add(cr[:, 1], cr[:, 0], 1.0))
                    step(nc.vector.tensor_scalar_mul(page_f[:, :], con("tok_row"), 2.0))
                    tr = row_base[:, 128:256].rearrange("p (r b) -> p r b", r=2)
                    step(nc.vector.tensor_scalar_add(tr[:, 0], pf[:, 4:68], page_f[:, :]))
                    step(nc.vector.tensor_scalar_add(tr[:, 1], tr[:, 0], 1.0))
            end_stage()

        page_f = sb("page_f", [128, 1])

        def nsa_places():
            P = Place()
            p = {}
            p["qT"] = P(2, GRP, T)
            p["gates"] = P(3, 48)
            p["kT_sel"] = P(2, T)
            p["kT_win"] = P(2, T)
            p["kc_p"] = P(2, N_CMP_P)
            p["kc_s"] = P(2, NB, N_CMP_S)
            p["vc_p"] = P(KV * HD)
            p["vc_s"] = P(NB, KV * HD)
            p["qpad"] = P(NB, 2, 32)
            p["pos"] = P(2)
            p["kv"] = P(3, 6 * KV * HD)
            p["rest"] = P
            return p

        def stage_nsa_in(l):
            L = l // 3
            p = nsa_places()
            P = p["rest"]
            wg = P(8, 48)
            n0 = st["used"]
            plan = planned([4, 4, 3, 3, 3], n0)
            np_ = len(plan)
            kv = p["kv"]
            with nc.Block() as block:
                @block.sync
                def _(sp):
                    loaded.on(sp.dma_start(wg, a["nsa_w_in"][L].rearrange("(k p) n -> p k n", p=128)[:, :, 2560:2608]), 16)
                    for b in range(NB):
                        stored2.on(sp.dma_start(win_s[L, b, 0:WIN - 1], a["cache_nsa_win"][L, b, 1:WIN]), 16)
                    stream(sp, 5)
                    sp.wait_ge(mm_taken.sem, mm_taken.at(np_))
                    stored.on(sp.dma_start(kv_p[L, 0].rearrange("(i p) r k d -> p i (r k d)", p=128),
                                           kv[:, 0:2, 0:1024]), 16)
                    stored.on(sp.dma_start(kv_s[L, :, 0].rearrange("b r k d -> b (r k d)"), kv[0:NB, 2, 0:1024]), 16)
                    stored.on(sp.dma_start(win_p[L, 0].rearrange("(i p) r k d -> p i (r k d)", p=128),
                                           kv[:, 0:2, 1024:1536]), 16)
                    stored.on(sp.dma_start(win_s[L, :, WIN - 1].rearrange("b r k d -> b (r k d)"),
                                           kv[0:NB, 2, 1024:1536]), 16)
                    sp.wait_ge(stored.sem, stored.at(64))

                @block.tensor
                def _(pe):
                    n = 0
                    for u in range(5):
                        w = unit(pe, n0 + u)
                        for m in range(4 if u < 2 else 3):
                            if n >= 4:
                                pe.wait_ge(mm_taken.sem, mm_taken.at(n - 3))
                            for k in range(8):
                                if u < 2:
                                    ins = nc.tensor.matmul(PS[:, n % 4, 0:T], w[:, k, m * 128:(m + 1) * 128],
                                                           hT[:, k, :], start=k == 0, stop=k == 7)
                                else:
                                    r = 128 if m < 2 else NB
                                    ins = nc.tensor.matmul(PS[0:r, n % 4, :], hT[:, k, m * 128:m * 128 + r],
                                                           w[:, k, :], start=k == 0, stop=k == 7)
                            plan[n][0].on(ins)
                            n += 1
                    pe.wait_ge(loaded.sem, loaded.at(16))
                    for m in range(3):
                        r = 128 if m < 2 else NB
                        for k in range(8):
                            ins = nc.tensor.matmul(PS[0:r, 4, m * 48:(m + 1) * 48], hT[:, k, m * 128:m * 128 + r],
                                                   wg[:, k, :], start=k == 0, stop=k == 7)
                        aux_ready.on(ins)
                    pe.wait_ge(mm_taken.sem, mm_taken.at(np_))
                    for j, c0 in enumerate((512, 640, 1024, 1152)):
                        b = j % 4
                        for m in range(3):
                            r = 128 if m < 2 else NB
                            ins = nc.tensor.transpose(PS[:, b, m * 128:m * 128 + r], kv[0:r, m, c0:c0 + 128],
                                                      ident[0:r, 0:r])
                        pt_ready.on(ins)

                @block.scalar
                def _(act):
                    for n in range(np_):
                        act.wait_ge(plan[n][0].sem, plan[n][1])
                        if n < 8:
                            half = 64 * (n // 2 % 2)
                            for e in range(2):
                                ins = nc.scalar.activation(p["qT"][half:half + 64, n // 4, 2 * (n % 2) + e, :],
                                                           PS[64 * e:64 * e + 64, n % 4, 0:T], ACT.Copy,
                                                           scale=HD ** -0.5)
                        else:
                            u, m = divmod(n - 8, 3)
                            r = 128 if m < 2 else NB
                            ins = nc.scalar.activation(kv[0:r, m, u * UC:(u + 1) * UC], PS[0:r, n % 4, :], ACT.Copy)
                        mm_taken.on(ins)
                    act.wait_ge(aux_ready.sem, aux_ready.at(3))
                    nc.scalar.activation(p["gates"][:, 0:2, :], PS[:, 4, 0:96].rearrange("p (m c) -> p m c", m=2),
                                         ACT.Sigmoid)
                    nc.scalar.activation(p["gates"][0:NB, 2, :], PS[0:NB, 4, 96:144], ACT.Sigmoid)

                @block.vector
                def _(v):
                    step = stepper(v, dve_step)
                    step(nc.vector.tensor_scalar_add(row_no[:, :], row_base[:, :], float(L * N_PHYS * PAGE * 4)))
                    step(nc.vector.memset(p["qpad"].rearrange("p b a c -> p (b a c)"), 0.0))
                    v.wait_ge(mm_taken.sem, mm_taken.at(8))
                    for par2 in range(2):
                        for at in range(2):
                            for h in range(2):
                                rows = slice(64 * h, 64 * h + 64)
                                dst = p["qpad"][rows, par2::2, at, par2 * 16 + 8 * at + 4 * h:par2 * 16 + 8 * at + 4 * h + 4]
                                src = p["qT"][rows, at, :, SEQ + par2:T:2].rearrange("p g b -> p b g")
                                nc.vector.tensor_copy(dst, src)
                    for j in range(4):
                        v.wait_ge(pt_ready.sem, pt_ready.at(j + 1))
                        dst = (p["kT_sel"], p["kT_win"])[j // 2]
                        nc.vector.tensor_copy(dst[:, j % 2, :], PS[:, j, 0:T])
            st["used"] += 5
            end_stage()

        def stage_nsa_compress(l):
            L = l // 3
            p = nsa_places()
            P = p["rest"]
            G = P(2, CMP, KV * HD)
            xt = P(8, 512)
            w2 = P(2, HD)
            hid = P(504)
            w1 = [hT[:, :, :].rearrange("p t n -> p (t n)")[:, 0:2048].rearrange("p (j e) -> p j e", j=16),
                  mT[:, :, :].rearrange("p t n -> p (t n)")[:, 0:2048].rearrange("p (j e) -> p j e", j=16)]
            order = [(r, g) for r in range(2) for g in (0, 1, 2, 3, 4)]
            rows = lambda g: 128 if g < 4 else SEQ // CMP
            count, fc = [0, 0], []
            for n, (r, g) in enumerate(order):
                count[n % 2] += 16 * (CMP if g < 4 else 1)
                fc.append(count[n % 2])

            def compressed(act, n):
                r, g = order[n]
                act.wait_ge(out_ready.sem, out_ready.at(n + 1))
                b = 2 + n % 2
                if r == 0:
                    src = PS[:, b, 0:256].rearrange("p (a n) -> p a n", a=2)
                    if g < 4:
                        ins = nc.scalar.activation(
                            p["kc_s"][:, :, 2 * g:2 * g + 2, :],
                            src[:, :, 0:126].rearrange("p a (b n) -> p a b n", b=2), ACT.Copy)
                    else:
                        ins = nc.scalar.activation(p["kc_p"], src[:, :, 0:N_CMP_P], ACT.Copy)
                elif g < 4:
                    ins = nc.scalar.activation(p["vc_s"][0:63, 2 * g:2 * g + 2, :],
                                               PS[0:63, b, :].rearrange("p (b n) -> p b n", b=2), ACT.Copy)
                else:
                    ins = nc.scalar.activation(p["vc_p"][0:N_CMP_P, :], PS[0:N_CMP_P, b, 0:256], ACT.Copy)
                out_taken.on(ins)

            def regroup(i, h, t):
                n, j = divmod(i, 8)
                R = rows(order[n][1])
                src = PS[64 * h:64 * h + 64, 4 + i % 2, t * 256:(t + 1) * 256].rearrange("p (a n) -> p a n", a=2)
                dst = xt[64 * t:64 * t + 64, j, :].rearrange("p (a k n) -> p a k n", a=2, k=2)[:, :, h]
                return dst[:, :, 0:R], src[:, :, 0:R]

            with nc.Block() as block:
                @block.sync
                def _(sp):
                    for r in range(2):
                        loaded.on(sp.dma_start(w1[r], a["nsa_cmp_w1"][L, r].rearrange("(j p) e -> p j e", p=128)), 16)
                    loaded.on(sp.dma_start(w2, a["nsa_cmp_w2"][L].rearrange("r e f -> e r f")), 16)

                @block.gpsimd
                def _(pool):
                    for n, (r, g) in enumerate(order):
                        if n >= 2:
                            pool.wait_ge(pt_ready.sem, pt_ready.at(8 * (n - 1)))
                        if g < 4:
                            for t in range(CMP):
                                fetched[n % 2].on(pool.indirect_dma_start(
                                    G[:, n % 2, t, :], None, cache_rows,
                                    bass.IndirectOffsetOnAxis(ap=cmp_rows[:, r, g, t:t + 1], axis=0)), 16)
                        else:
                            src = kv_p[L, 0].rearrange("(c t) r k d -> c t r (k d)", t=CMP)[:, :, r, :]
                            fetched[n % 2].on(pool.dma_start(G[0:SEQ // CMP, n % 2, :, :], src), 16)

                @block.tensor
                def _(pe):
                    pe.wait_ge(loaded.sem, loaded.at(48))
                    for r in range(2):
                        for j in range(16):
                            ins = nc.tensor.matmul(PS[:, 6, r:r + 1], w1[r][:, j, :], cmp_pos[:, L, r, j:j + 1],
                                                   start=j == 0, stop=j == 15)
                    aux_ready.on(ins)

                    def turn(n, j):
                        i = 8 * n + j
                        R = rows(order[n][1])
                        if i >= 2:
                            pe.wait_ge(pt_taken.sem, pt_taken.at(i - 1))
                            pe.wait_ge(pt_taken2.sem, pt_taken2.at(i - 1))
                        for t in range(2):
                            for at in range(2):
                                o = (2 * t + at) * 128
                                ins = nc.tensor.transpose(PS[:, 4 + i % 2, o:o + R],
                                                          G[0:R, n % 2, 2 * j + t, at * 128:(at + 1) * 128],
                                                          ident[0:R, 0:R])
                        pt_ready.on(ins)

                    def out(n):
                        r, g = order[n]
                        pe.wait_ge(given.sem, given.at(n + 1))
                        if n >= 2:
                            pe.wait_ge(out_taken.sem, out_taken.at(n - 1))
                        b = 2 + n % 2
                        if r == 0:
                            m = 126 if g < 4 else N_CMP_P
                            for k in range(KV):
                                ins = nc.tensor.matmul(
                                    PS[64 * (k % 2):64 * (k % 2) + 64, b, (k // 2) * 128:(k // 2) * 128 + m],
                                    w2[:, 0, :], hid[:, k * m:(k + 1) * m], start=True, stop=True)
                        elif g < 4:
                            for k in range(KV):
                                for i in range(2):
                                    ins = nc.tensor.matmul(PS[0:63, b, (i * 4 + k) * 64:(i * 4 + k + 1) * 64],
                                                           hid[:, (2 * k + i) * 63:(2 * k + i + 1) * 63], w2[:, 1, :],
                                                           start=True, stop=True)
                        else:
                            for k in range(KV):
                                ins = nc.tensor.matmul(PS[0:N_CMP_P, b, k * 64:(k + 1) * 64],
                                                       hid[:, k * N_CMP_P:(k + 1) * N_CMP_P], w2[:, 1, :],
                                                       start=True, stop=True)
                        out_ready.on(ins)

                    pe.wait_ge(fetched[0].sem, fetched[0].at(fc[0]))
                    for j in range(8):
                        turn(0, j)
                    for n, (r, g) in enumerate(order):
                        if n + 1 < len(order):
                            pe.wait_ge(fetched[(n + 1) % 2].sem, fetched[(n + 1) % 2].at(fc[n + 1]))
                        for j in range(8):
                            pe.wait_ge(pt_taken.sem, pt_taken.at(8 * n + j + 1))
                            pe.wait_ge(pt_taken2.sem, pt_taken2.at(8 * n + j + 1))
                            for h in range(2):
                                if g < 4:
                                    x = xt[:, j, :].rearrange("p (c n) -> p c n", n=64)[:, :, h:h + 63]
                                    o = PS[:, n % 2, 0:504]
                                else:
                                    x = xt[:, j, :].rearrange("p (c n) -> p c n", n=128)[:, :, h:h + N_CMP_P]
                                    o = PS[:, n % 2, 0:KV * N_CMP_P]
                                ins = nc.tensor.matmul(o, w1[r][:, 8 * h + j, :], x, start=j == 0 and h == 0,
                                                       stop=j == 7 and h == 1)
                            if j == 7:
                                mm_ready.on(ins)
                            if n + 1 < len(order):
                                turn(n + 1, j)
                            if j == 3 and n:
                                out(n - 1)
                    out(len(order) - 1)

                @block.vector
                def _(v):
                    v.wait_ge(aux_ready.sem, aux_ready.at(1))
                    aux_taken.on(nc.vector.tensor_copy(p["pos"], PS[:, 6, 0:2]))
                    for i in range(8 * len(order)):
                        v.wait_ge(pt_ready.sem, pt_ready.at(i + 1))
                        for t in range(2):
                            dst, src = regroup(i, 0, t)
                            ins = nc.vector.tensor_copy(dst, src)
                        pt_taken.on(ins)

                @block.scalar
                def _(act):
                    def regroups(i0, i1):
                        for i in range(i0, min(i1, 8 * len(order))):
                            act.wait_ge(pt_ready.sem, pt_ready.at(i + 1))
                            for t in range(2):
                                dst, src = regroup(i, 1, t)
                                ins = nc.scalar.activation(dst, src, ACT.Copy)
                            pt_taken2.on(ins)

                    regroups(0, 8)
                    act.wait_ge(aux_taken.sem, aux_taken.at(1))
                    for n, (r, g) in enumerate(order):
                        regroups(8 * n + 8, 8 * n + 12)
                        if n:
                            compressed(act, n - 1)
                        regroups(8 * n + 12, 8 * n + 16)
                        m = 504 if g < 4 else KV * N_CMP_P
                        act.wait_ge(mm_ready.sem, mm_ready.at(n + 1))
                        given.on(nc.scalar.activation(hid[:, 0:m], PS[:, n % 2, 0:m], ACT.Gelu_apprx_tanh,
                                                      bias=p["pos"][:, r:r + 1]))
                    compressed(act, len(order) - 1)
            end_stage()

        def stage_nsa_prompt(l):
            p = nsa_places()
            P = p["rest"]
            kv, gates = p["kv"], p["gates"]
            mats = P(2, HEADS, 128)
            bcmp = P(2, HEADS, N_CMP_P)
            S = P(2, GRP, 2, 256)
            Sc = P(2, GRP, 16)
            small = P(2, 3, GRP * 3)
            PT = P(GRP, 4, 128)
            PTc = P(GRP, 128)
            groups = [(k, i) for k in range(KV) for i in range(2)]
            cmul = con("cmp_mul").rearrange("p (i n) -> p i n", i=2)
            view = lambda n, j: small[:, n % 2, j, :].rearrange("p (g r) -> p g r", g=GRP)
            with nc.Block() as block:
                @block.sync
                def _(sp):
                    nb = 2 * HEADS * 128
                    loaded.on(sp.dma_start(mats.rearrange("p a b c -> p (a b c)"), bias_dram[:, 0:nb]), 16)
                    loaded.on(sp.dma_start(bcmp.rearrange("p a b c -> p (a b c)"), bias_dram[:, nb:]), 16)

                @block.tensor
                def _(pe):
                    def scores(n):
                        k, i = groups[n]
                        rows, nk, at = slice(64 * (k % 2), 64 * (k % 2) + 64), 128 * (i + 1), k // 2
                        if n:
                            pe.wait_ge(scores_taken.sem, scores_taken.at(n))
                        for g in range(GRP):
                            q = p["qT"][rows, at, g, i * 128:(i + 1) * 128]
                            nc.tensor.matmul(PS[:, g, 0:nk], q, p["kT_sel"][rows, at, 0:nk], start=True, stop=True)
                            nc.tensor.matmul(PS[:, g, 256:256 + nk], q, p["kT_win"][rows, at, 0:nk],
                                             start=True, stop=True)
                        if n >= 2:
                            pe.wait_ge(pt_taken.sem, pt_taken.at(5 * (n - 1)))
                        for g in range(GRP):
                            ins = nc.tensor.matmul(PS[:, 4, g * 16:g * 16 + N_CMP_P],
                                                   p["qT"][rows, at, g, i * 128:(i + 1) * 128],
                                                   p["kc_p"][rows, at, :], start=True, stop=True)
                        scores_ready.on(ins)

                    scores(0)
                    scores(1)
                    for n, (k, i) in enumerate(groups):
                        pe.wait_ge(probs_ready.sem, probs_ready.at(n + 1))
                        for g in range(GRP):
                            if g >= 2:
                                pe.wait_ge(pt_taken.sem, pt_taken.at(5 * n + g - 1))
                            for r in range(2):
                                for kt in range(i + 1):
                                    ins = nc.tensor.transpose(
                                        PS[:, 5 + g % 2, (2 * r + kt) * 128:(2 * r + kt + 1) * 128],
                                        S[:, n % 2, g, r, kt * 128:(kt + 1) * 128], ident)
                            pt_ready.on(ins)
                        for g in range(GRP):
                            ins = nc.tensor.transpose(PS[0:N_CMP_P, 4, g * 128:(g + 1) * 128],
                                                      Sc[:, n % 2, g, 0:N_CMP_P], ident)
                        pt_ready.on(ins)
                        if n + 2 < len(groups):
                            scores(n + 2)
                        pe.wait_ge(pt_taken.sem, pt_taken.at(5 * n + 5))
                        if n:
                            pe.wait_ge(out_taken.sem, out_taken.at(n))
                        for g in range(GRP):
                            o = PS[64 * (g % 2):64 * (g % 2) + 64, 7, (g // 2) * 128:128 + (g // 2) * 128]
                            nc.tensor.matmul(o, p["vc_p"][0:N_CMP_P, k * HD:(k + 1) * HD], PTc[0:N_CMP_P, g, :],
                                             start=True, stop=False)
                            for r in range(2):
                                for kt in range(i + 1):
                                    c0 = (768, 1280)[r] + k * HD
                                    ins = nc.tensor.matmul(o, kv[:, kt, c0:c0 + HD], PT[:, g, 2 * r + kt, :],
                                                           start=False, stop=r == 1 and kt == i)
                        out_ready.on(ins)

                @block.vector
                def _(v):
                    step = stepper(v, dve_step)
                    v.wait_ge(loaded.sem, loaded.at(32))

                    def logits(n):
                        k, i = groups[n]
                        b = n % 2
                        v.wait_ge(scores_ready.sem, scores_ready.at(n + 1))
                        if n >= 2:
                            v.wait_ge(pt_ready.sem, pt_ready.at(5 * (n - 1)))
                        for kt in range(i + 1):
                            src = PS[:, 0:4, :].rearrange("p g (r n) -> p g r n", r=2)[:, :, :, kt * 128:(kt + 1) * 128]
                            m = mats[:, i - kt, 4 * k:4 * k + 4, :]
                            nc.vector.tensor_tensor(S[:, b, :, :, kt * 128:(kt + 1) * 128], src, bc(m, 2, 2), ALU.add)
                        src = PS[:, 4, 0:64].rearrange("p (g n) -> p g n", g=GRP)[:, :, 0:N_CMP_P]
                        step(nc.vector.tensor_tensor(Sc[:, b, :, 0:N_CMP_P], src, bcmp[:, i, 4 * k:4 * k + 4, :], ALU.add))
                        v.sem_inc(scores_taken.sem, 1)
                        scores_taken.given += 1
                        nk = 128 * (i + 1)
                        mx = view(n, 0)
                        nc.vector.tensor_reduce(mx[:, :, 1:3], S[:, b, :, :, 0:nk], AX.X, ALU.max)
                        step(nc.vector.tensor_reduce(mx[:, :, 0:1], Sc[:, b, :, 0:N_CMP_P], AX.X, ALU.max))
                        max_ready.on(nc.vector.tensor_scalar_mul(small[:, b, 0, :], small[:, b, 0, :], -1.0))

                    logits(0)
                    logits(1)
                    for n, (k, i) in enumerate(groups):
                        b, nk = n % 2, 128 * (i + 1)
                        sums, fac = view(n, 1), view(n, 2)
                        v.wait_ge(exp_ready.sem, exp_ready.at(n + 1))
                        c = Sc[:, b, :, 0:N_CMP_P]
                        step(nc.vector.tensor_tensor(c, c, bc(cmul[:, i], 1, GRP), ALU.mult))
                        step(nc.vector.tensor_reduce(sums[:, :, 0:1], c, AX.X, ALU.add))
                        step(nc.vector.tensor_scalar_max(small[:, b, 1, :], small[:, b, 1, :], 1e-30))
                        step(nc.vector.reciprocal(small[:, b, 1, :], small[:, b, 1, :]))
                        gt = gates[:, i, :].rearrange("p (r k g) -> p k g r", r=3, k=KV)[:, k]
                        step(nc.vector.tensor_tensor(fac, sums, gt, ALU.mult))
                        s = S[:, b, :, :, 0:nk]
                        nc.vector.tensor_tensor(s, s, bc(fac[:, :, 1:3], 3, nk), ALU.mult)
                        probs_ready.on(nc.vector.tensor_tensor(c, c, fac[:, :, 0:1].broadcast_to([128, GRP, N_CMP_P]),
                                                               ALU.mult))
                        for g in range(GRP):
                            v.wait_ge(pt_ready.sem, pt_ready.at(5 * n + g + 1))
                            src = PS[:, 5 + g % 2, :].rearrange("p (r n) -> p r n", r=2)[:, :, 0:nk]
                            dst = PT[:, g, :, :].rearrange("p b n -> p (b n)").rearrange("p (r n) -> p r n", r=2)[:, :, 0:nk]
                            pt_taken.on(nc.vector.tensor_copy(dst, src))
                        v.wait_ge(pt_ready.sem, pt_ready.at(5 * n + 5))
                        pt_taken.on(nc.vector.tensor_copy(PTc[0:N_CMP_P].rearrange("p g n -> p (g n)"),
                                                          PS[0:N_CMP_P, 4, :]))
                        if n + 2 < len(groups):
                            logits(n + 2)

                @block.scalar
                def _(act):
                    step = stepper(act, act_step)

                    def exps(n):
                        k, i = groups[n]
                        b, nk = n % 2, 128 * (i + 1)
                        act.wait_ge(max_ready.sem, max_ready.at(n + 1))
                        for g in range(GRP):
                            for r in range(2):
                                s = S[:, b, g, r, 0:nk]
                                nc.scalar.activation(s, s, ACT.Exp, bias=view(n, 0)[:, g, 1 + r:2 + r],
                                                     accum_out=view(n, 1)[:, g, 1 + r:2 + r])
                            c = Sc[:, b, g, 0:N_CMP_P]
                            ins = nc.scalar.activation(c, c, ACT.Exp, bias=view(n, 0)[:, g, 0:1])
                        exp_ready.on(ins)

                    exps(0)
                    exps(1)
                    for n, (k, i) in enumerate(groups):
                        act.wait_ge(out_ready.sem, out_ready.at(n + 1))
                        out_taken.on(nc.scalar.activation(
                            hT[:, 2 * k:2 * k + 2, i * 128:(i + 1) * 128],
                            PS[:, 7, 0:256].rearrange("p (t n) -> p t n", t=2), ACT.Copy))
                        if n + 2 < len(groups):
                            exps(n + 2)
            end_stage()

        def stage_nsa_sample(l):
            L = l // 3
            p = nsa_places()
            kv, gates = p["kv"], p["gates"]
            P = Place(p["rest"].at - 3 * 6 * KV * HD)
            kw = P(4, KV * HD)
            ktw = P(2, WIN)
            PT = P(13, 32)
            Sc = P(66, rows=32)
            imp = P(64, rows=32)
            misc = P(64, rows=32)
            gr = P(12, rows=32)
            new = P(2, 32, rows=32)
            pn = P(64, rows=NB)
            gtmp = P(12, 16, rows=32)
            relb = P(2 * HEADS, rows=32)
            assert P.at <= p["rest"].at - 6 * KV * HD
            P = Place(p["rest"].at)
            V = P(2, PAGES, KV * HD)
            vw = P(2, 4, KV * HD)
            K = P(2, PAGES, KV * HD)
            S = P(1026, rows=32)
            Sw = P(514, rows=32)
            oh = P(1090, rows=32)
            KT = mT[:, :, :].rearrange("p t n -> p (t n)")[:, 0:2048].rearrange("p (a n) -> p a n", a=2)
            win = a["cache_nsa_win"]
            o0 = NARROW_AT["past"][0]
            with nc.Block() as block:
                @block.sync
                def _(sp):
                    loaded.on(sp.dma_start(oh, consts[1][:, o0:o0 + 1090]), 16)
                    for i in range(2):
                        loaded.on(sp.dma_start(relb[:, i * HEADS:(i + 1) * HEADS], a["rel_bias"]), 16)
                    for b in range(NB):
                        if b:
                            sp.wait_ge(pt_ready.sem, pt_ready.at(6 * b))
                        loaded2.on(sp.dma_start(kw, win[L, b, :, 0].rearrange("(i p) k d -> p i (k d)", p=128)), 16)
                        if b >= 2 and b % 2 == 0:
                            sp.wait_ge(out_ready.sem, out_ready.at(b // 2))
                        fetched_w.on(sp.dma_start(vw[:, b % 2], win[L, b, :, 1].rearrange("(i p) k d -> p i (k d)", p=128)), 16)

                @block.gpsimd
                def _(pool):
                    for b in range(NB):
                        if b >= 2:
                            pool.wait_ge(pt_ready.sem, pt_ready.at(6 * (b - 1)))
                        for j in range(PAGES):
                            fetched[b % 2].on(pool.indirect_dma_start(
                                K[:, b % 2, j, :], None, cache_rows,
                                bass.IndirectOffsetOnAxis(ap=tok_rows[:, 0, b * PAGES + j:b * PAGES + j + 1], axis=0)), 16)
                        if b >= 2 and b % 2 == 0:
                            pool.wait_ge(out_ready.sem, out_ready.at(b // 2))
                        for j in range(PAGES):
                            fetched[2 + b % 2].on(pool.indirect_dma_start(
                                V[:, b % 2, j, :], None, cache_rows,
                                bass.IndirectOffsetOnAxis(ap=tok_rows[:, 1, b * PAGES + j:b * PAGES + j + 1], axis=0)), 16)

                @block.tensor
                def _(pe):
                    pe.wait_ge(loaded.sem, loaded.at(48))
                    rows = con("sample_rows", NB).rearrange("p (g r) -> p g r", g=4)
                    for g in range(4):
                        ins = nc.tensor.matmul(PS[0:32, 7, g * 48:(g + 1) * 48], rows[:, g, :], gates[0:NB, 2, :],
                                               start=True, stop=True)
                    aux_ready.on(ins)

                    def turn(b, x):
                        i = 6 * b + x
                        if i >= 2:
                            pe.wait_ge(pt_taken.sem, pt_taken.at(i - 1))
                        if x == 0:
                            pe.wait_ge(fetched[b % 2].sem, fetched[b % 2].at(128 * (b // 2 + 1)))
                        if x == 4:
                            pe.wait_ge(loaded2.sem, loaded2.at(16 * (b + 1)))
                        for j in range(4):
                            if x < 4:
                                src = K[:, b % 2, 4 * (x % 2) + j, (x // 2) * 128:(x // 2 + 1) * 128]
                            else:
                                src = kw[:, j, (x - 4) * 128:(x - 3) * 128]
                            ins = nc.tensor.transpose(PS[:, 5 + i % 2, j * 128:(j + 1) * 128], src, ident)
                        pt_ready.on(ins)

                    def score(b, x):
                        i = 6 * b + x
                        pe.wait_ge(pt_taken.sem, pt_taken.at(i + 1))
                        at = x // 2 if x < 4 else x - 4
                        q = p["qpad"][:, b, at, :]
                        last = b % 2 == 1 and at == 1
                        if x < 4:
                            return nc.tensor.matmul(PS[0:32, x % 2, :], q, KT[:, at, (x % 2) * 512:(x % 2 + 1) * 512],
                                                    start=False, stop=last)
                        return nc.tensor.matmul(PS[0:32, 2, :], q, ktw[:, at, :], start=False, stop=last)

                    for g in range(4):
                        if g:
                            pe.wait_ge(scores_taken.sem, scores_taken.at(g))
                        rb = relb
                        for bank, c0, n in ((0, 0, 512), (1, 512, 512), (2, 512, 512), (3, 1024, 66)):
                            nc.tensor.matmul(PS[0:32, bank, 0:n], rb, oh[:, c0:c0 + n], start=True, stop=False)
                        for b in (2 * g, 2 * g + 1):
                            for at in range(2):
                                q = p["qpad"][:, b, at, :]
                                last = b % 2 == 1 and at == 1
                                nc.tensor.matmul(PS[0:32, 3, 0:N_CMP_S], q, p["kc_s"][:, at, b, :], start=False, stop=False)
                                nc.tensor.matmul(PS[0:32, 3, 64:65], q, p["kT_sel"][:, at, SEQ + b:SEQ + b + 1],
                                                 start=False, stop=False)
                                nc.tensor.matmul(PS[0:32, 3, 65:66], q, p["kT_win"][:, at, SEQ + b:SEQ + b + 1],
                                                 start=False, stop=last)
                            turn(b, 0)
                            for x in range(6):
                                if x < 5:
                                    turn(b, x + 1)
                                ins = score(b, x)
                        scores_ready.on(ins)
                        pe.wait_ge(imp_ready.sem, imp_ready.at(g + 1))
                        aux_ready.on(nc.tensor.matmul(PS[0:32, 7, 0:N_CMP_S], con("group_sum", 32), Sc[:, 0:N_CMP_S],
                                                      start=True, stop=True))
                        pe.wait_ge(probs_ready.sem, probs_ready.at(g + 1))
                        for j in range(12):
                            src = S[:, j * 128:(j + 1) * 128] if j < 8 else Sw[:, (j - 8) * 128:(j - 7) * 128]
                            nc.tensor.transpose(PS[:, 4, j * 32:(j + 1) * 32], src, ident[0:32, 0:32])
                        nc.tensor.transpose(PS[0:N_CMP_S, 4, 384:416], Sc[:, 0:N_CMP_S], ident[0:32, 0:32])
                        rs = con("row_sample", 32).rearrange("p (g b) -> p g b", g=4)
                        aux_ready.on(nc.tensor.matmul(PS[0:NB, 7, 128:192], rs[:, g, :], new.rearrange("p a n -> p (a n)"),
                                                      start=True, stop=True))
                        pe.wait_ge(aux_taken.sem, aux_taken.at(g + 1))
                        for f in (2, 3):
                            pe.wait_ge(fetched[f].sem, fetched[f].at(128 * (g + 1)))
                        pe.wait_ge(fetched_w.sem, fetched_w.at(32 * (g + 1)))
                        for at in range(2):
                            for b2 in range(2):
                                o = PS[:, 7, 256 + (at * 2 + b2) * 8:264 + (at * 2 + b2) * 8]
                                c = slice(b2 * 16 + 8 * at, b2 * 16 + 8 * at + 8)
                                cv = slice(at * 128, (at + 1) * 128)
                                nc.tensor.matmul(o, p["vc_s"][0:N_CMP_S, 2 * g + b2, cv], PT[0:N_CMP_S, 12, c],
                                                 start=True, stop=False)
                                for j in range(PAGES):
                                    nc.tensor.matmul(o, V[:, b2, j, cv], PT[:, j, c], start=False, stop=False)
                                for j in range(4):
                                    nc.tensor.matmul(o, vw[:, b2, j, cv], PT[:, 8 + j, c], start=False, stop=False)
                                nc.tensor.matmul(o, kv[0:NB, 2, 768 + at * 128:896 + at * 128], pn[:, c],
                                                 start=False, stop=False)
                                ins = nc.tensor.matmul(o, kv[0:NB, 2, 1280 + at * 128:1408 + at * 128],
                                                       pn[:, 32 + b2 * 16 + 8 * at:32 + b2 * 16 + 8 * at + 8],
                                                       start=False, stop=True)
                        out_ready.on(ins)

                @block.vector
                def _(v):
                    step = stepper(v, dve_step)
                    v.wait_ge(aux_ready.sem, aux_ready.at(1))
                    step(nc.vector.tensor_tensor(gtmp, PS[0:32, 7, 0:192].rearrange("p (a h) -> p a h", a=12),
                                                 bc(con("pick_head", 32), 1, 12), ALU.mult))
                    step(nc.vector.tensor_reduce(gr, gtmp, AX.X, ALU.add))
                    for g in range(4):
                        for i in range(12 * g, 12 * g + 12):
                            x = i % 6
                            v.wait_ge(pt_ready.sem, pt_ready.at(i + 1))
                            dst = KT[:, x // 2, (x % 2) * 512:(x % 2 + 1) * 512] if x < 4 else ktw[:, x - 4, :]
                            pt_taken.on(nc.vector.tensor_copy(dst, PS[:, 5 + i % 2, :]))
                        v.wait_ge(scores_ready.sem, scores_ready.at(g + 1))
                        step(nc.vector.tensor_copy(Sc, PS[0:32, 3, 0:66]))
                        nm, sm, fc = misc[:, 0:3], misc[:, 4:7], misc[:, 8:11]
                        low, eq, drop, top = misc[:, 12:13], misc[:, 16:30], misc[:, 32:46], misc[:, 13:14]
                        score = misc[:, 48:62]
                        step(nc.vector.tensor_reduce(nm[:, 0:1], Sc[:, 0:N_CMP_S], AX.X, ALU.max))
                        max_ready.on(nc.vector.tensor_scalar_mul(nm[:, 0:1], nm[:, 0:1], -1.0))
                        v.wait_ge(exp_ready.sem, exp_ready.at(2 * g + 1))
                        step(nc.vector.reciprocal(sm[:, 0:1], sm[:, 0:1]))
                        imp_ready.on(nc.vector.tensor_scalar_mul(Sc[:, 0:N_CMP_S], Sc[:, 0:N_CMP_S], sm[:, 0:1]))
                        v.wait_ge(aux_ready.sem, aux_ready.at(2 + 2 * g))
                        step(nc.vector.tensor_copy(imp[:, 0:N_CMP_S], PS[0:32, 7, 0:N_CMP_S]))
                        step(nc.vector.tensor_tensor(imp[:, 3:59], imp[:, 4:60], imp[:, 3:59], ALU.add))
                        step(nc.vector.tensor_scalar_mul(imp[:, 3:59], imp[:, 3:59], 0.5))
                        step(nc.vector.tensor_reduce(score, imp[:, 3:59].rearrange("p (s i) -> p s i", i=4), AX.X, ALU.add))
                        step(nc.vector.tensor_reduce(low, score, AX.X, ALU.min))
                        step(nc.vector.tensor_scalar(eq, score, low, None, ALU.is_equal))
                        step(nc.vector.tensor_tensor(eq, eq, con("block_no", 32), ALU.mult))
                        step(nc.vector.tensor_reduce(top, eq, AX.X, ALU.max))
                        step(nc.vector.tensor_scalar(drop, con("block_no", 32), top, NEG, ALU.is_equal, ALU.mult))
                        ps = PS[0:32, 0:2, :].rearrange("p b n -> p (b n)")
                        step(nc.vector.tensor_tensor(S[:, 64:960].rearrange("p (s n) -> p s n", n=64),
                                                     ps[:, 64:960].rearrange("p (s n) -> p s n", n=64),
                                                     bc(drop, 2, 64), ALU.add))
                        nc.vector.tensor_copy(S[:, 0:64], ps[:, 0:64])
                        nc.vector.tensor_copy(S[:, 960:1024], ps[:, 960:1024])
                        nc.vector.tensor_copy(S[:, 1024:1025], Sc[:, 64:65])
                        nc.vector.tensor_copy(Sw[:, 512:513], Sc[:, 65:66])
                        step(nc.vector.tensor_copy(Sw[:, 0:512], PS[0:32, 2, :]))
                        v.sem_inc(scores_taken.sem, 1)
                        scores_taken.given += 1
                        step(nc.vector.tensor_reduce(nm[:, 1:2], S[:, 0:1025], AX.X, ALU.max))
                        step(nc.vector.tensor_reduce(nm[:, 2:3], Sw[:, 0:513], AX.X, ALU.max))
                        max_ready.on(nc.vector.tensor_scalar_mul(nm[:, 1:3], nm[:, 1:3], -1.0))
                        v.wait_ge(exp_ready.sem, exp_ready.at(2 * g + 2))
                        step(nc.vector.reciprocal(sm[:, 1:3], sm[:, 1:3]))
                        gg = gr[:, 3 * g:3 * g + 3]
                        step(nc.vector.tensor_tensor(fc[:, 1:3], sm[:, 1:3], gg[:, 1:3], ALU.mult))
                        step(nc.vector.tensor_scalar_mul(S[:, 0:1025], S[:, 0:1025], fc[:, 1:2]))
                        step(nc.vector.tensor_scalar_mul(Sw[:, 0:513], Sw[:, 0:513], fc[:, 2:3]))
                        step(nc.vector.tensor_scalar_mul(Sc[:, 0:N_CMP_S], Sc[:, 0:N_CMP_S], gg[:, 0:1]))
                        step(nc.vector.tensor_scalar_mul(new[:, 0, :], ident[0:32, 0:32], S[:, 1024:1025]))
                        probs_ready.on(nc.vector.tensor_scalar_mul(new[:, 1, :], ident[0:32, 0:32], Sw[:, 512:513]))
                        v.wait_ge(aux_ready.sem, aux_ready.at(3 + 2 * g))
                        nc.vector.tensor_copy(PT[:, 0:12, :].rearrange("p j n -> p (j n)"), PS[:, 4, 0:384])
                        nc.vector.tensor_copy(PT[0:N_CMP_S, 12, :], PS[0:N_CMP_S, 4, 384:416])
                        aux_taken.on(nc.vector.tensor_copy(pn, PS[0:NB, 7, 128:192]))
                        v.wait_ge(out_ready.sem, out_ready.at(g + 1))
                        o = PS[:, 7, 256:288].rearrange("p (a b h) -> p a b h", a=2, b=2)
                        for h in range(2):
                            for q in range(2):
                                src = o[64 * h:64 * h + 64, :, :, 4 * h + q:4 * h + q + 3:2]
                                dst = hT[64 * q:64 * q + 64, :, SEQ + 2 * g:SEQ + 2 * g + 2]\
                                    .rearrange("p (a t) b -> p a b t", a=2)[:, :, :, 2 * h:2 * h + 2]
                                step(nc.vector.tensor_copy(dst, src))

                @block.scalar
                def _(act):
                    nm, sm = misc[:, 0:3], misc[:, 4:7]
                    for g in range(4):
                        act.wait_ge(max_ready.sem, max_ready.at(2 * g + 1))
                        c = Sc[:, 0:N_CMP_S]
                        exp_ready.on(nc.scalar.activation(c, c, ACT.Exp, bias=nm[:, 0:1], accum_out=sm[:, 0:1]))
                        act.wait_ge(max_ready.sem, max_ready.at(2 * g + 2))
                        nc.scalar.activation(S[:, 0:1025], S[:, 0:1025], ACT.Exp, bias=nm[:, 1:2], accum_out=sm[:, 1:2])
                        exp_ready.on(nc.scalar.activation(Sw[:, 0:513], Sw[:, 0:513], ACT.Exp, bias=nm[:, 2:3],
                                                          accum_out=sm[:, 2:3]))
            end_stage()

        fetched_w = signal("fetched_w")

        def stage_project(src, depth):
            n0 = st["used"]
            with nc.Block() as block:
                @block.sync
                def _(sp):
                    stream(sp, 2 * depth)

                @block.tensor
                def _(pe):
                    for h in range(2):
                        for d in range(depth):
                            w = unit(pe, n0 + h * depth + d)
                            for m in range(4):
                                for k in range(8):
                                    ins = nc.tensor.matmul(PS[:, 4 * h + m, 0:T], w[:, k, m * 128:(m + 1) * 128],
                                                           src[:, 8 * d + k, :], start=d == 0 and k == 0,
                                                           stop=d == depth - 1 and k == 7)
                            w_used.on(ins)

                @block.scalar
                def _(act):
                    for h in range(2):
                        act.wait_ge(w_used.sem, n0 + (h + 1) * depth)
                        for m in range(4):
                            nc.scalar.activation(mT[:, 4 * h + m, :], PS[:, 4 * h + m, 0:T], ACT.Copy)
            st["used"] += 2 * depth
            end_stage()

        def mixer_nsa(l):
            stage_nsa_in(l)
            stage_nsa_compress(l)
            stage_nsa_prompt(l)
            stage_nsa_sample(l)
            stage_project(hT, 1)

        def stage_in(l, W, plan_units, take, act_extra=None):
            n0 = st["used"]
            per = [4 if u == "fm" else 3 for u in plan_units]
            plan = planned(per, n0)
            with nc.Block() as block:
                @block.sync
                def _(sp):
                    if act_extra:
                        act_extra["sync"](sp)
                    stream(sp, len(plan_units))

                @block.tensor
                def _(pe):
                    n = 0
                    for u, kind in enumerate(plan_units):
                        w = unit(pe, n0 + u)
                        for m in range(per[u]):
                            if n >= 4:
                                pe.wait_ge(mm_taken.sem, mm_taken.at(n - 3))
                            for k in range(8):
                                if kind == "fm":
                                    ins = nc.tensor.matmul(PS[:, n % 4, 0:T], w[:, k, m * 128:(m + 1) * 128],
                                                           hT[:, k, :], start=k == 0, stop=k == 7)
                                else:
                                    r = 128 if m < 2 else NB
                                    ins = nc.tensor.matmul(PS[0:r, n % 4, :], hT[:, k, m * 128:m * 128 + r],
                                                           w[:, k, :], start=k == 0, stop=k == 7)
                            plan[n][0].on(ins)
                            n += 1
                    if act_extra:
                        act_extra["tensor"](pe)

                @block.scalar
                def _(act):
                    n = 0
                    for u, kind in enumerate(plan_units):
                        for m in range(per[u]):
                            act.wait_ge(plan[n][0].sem, plan[n][1])
                            r = T if kind == "fm" else 512
                            rows = 128 if kind == "fm" or m < 2 else NB
                            mm_taken.on(take(u, m, PS[0:rows, n % 4, 0:r], rows))
                            n += 1
                    if act_extra:
                        act_extra["scalar"](act)
            st["used"] += len(plan_units)
            end_stage()

        def mixer_hgrn(l):
            P = Place()
            q = P(HG_H, T)
            f = P(HG_H, T)
            g = P(HG_H, T)
            k = P(HG_H, T)
            v_tok = P(3, D)
            cum = P(HG_H, SEQ)
            A = P(2, HG_H, 128)
            A2 = P(HG_H, 128)
            after_A = P.at
            qd = P(2, HG_H, SEQ)
            kd = P(2, HG_H, SEQ)
            om = P(DT)
            E = mT[:, :, :].rearrange("p t n -> p (t n)")[:, 0:2048].rearrange("p (h n) -> p h n", h=HG_H)

            def take(u, m, ps, rows):
                if u < 2:
                    return nc.scalar.activation(q[:, 4 * u + m, :], ps, ACT.Silu)
                if u < 4:
                    return nc.scalar.activation(f[:, 4 * (u - 2) + m, :], ps, ACT.Sigmoid)
                if u < 6:
                    return nc.scalar.activation(v_tok[0:rows, m, (u - 4) * UC:(u - 3) * UC], ps, ACT.Copy)
                return nc.scalar.activation(g[:, 4 * (u - 6) + m, :], ps, ACT.Silu)

            stage_in(l, None, ["fm"] * 4 + ["tok"] * 2 + ["fm"] * 2, take)

            levels = [(128, None)] + [(m, i) for i, m in enumerate(LEVELS)]
            masks = con("levels").rearrange("p (l n) -> p l n", l=len(LEVELS) + 1)

            def halves(x, m):
                return x.rearrange("p h (b two m) -> p h b two m", two=2, m=m)

            with nc.Block() as block:
                @block.vector
                def _(v):
                    step = stepper(v, dve_step)
                    step(nc.vector.tensor_scalar(om, lower[:, :], -1.0, 1.0, ALU.mult, ALU.add))
                    for h in range(HG_H):
                        step(nc.vector.tensor_scalar(f[:, h, :], f[:, h, :], om[:, h:h + 1], lower[:, h:h + 1],
                                                     ALU.mult, ALU.add))
                    given.on(nc.vector.tensor_scalar(k, f, -1.0, 1.0, ALU.mult, ALU.add))
                    nc.vector.memset(A.rearrange("p i h n -> p (i h n)"), 0.0)
                    nc.vector.memset(qd.rearrange("p i h n -> p (i h n)"), 0.0)
                    step(nc.vector.memset(kd.rearrange("p i h n -> p (i h n)"), 0.0))
                    v.wait_ge(act_step.sem, act_step.at(1))
                    for h in range(HG_H):
                        ins = nc.vector.tensor_tensor_scan(cum[:, h, :], ones[:, :], E[:, h, :], 0.0, ALU.mult, ALU.add)
                    step(ins)

                    def exponents(n):
                        m = levels[n][0]
                        c, e = halves(cum, m), halves(E, m)
                        anchor = c[:, :, :, 0, m - 1:m].broadcast_to([128, HG_H, 128 // m, m])
                        nc.vector.tensor_tensor(e[:, :, :, 1, :], c[:, :, :, 1, :], anchor, ALU.subtract)
                        max_ready.on(nc.vector.tensor_tensor(e[:, :, :, 0, :], anchor, c[:, :, :, 0, :], ALU.subtract))

                    exponents(0)
                    for n, (m, i) in enumerate(levels):
                        v.wait_ge(exp_ready.sem, exp_ready.at(n + 1))
                        if n >= 2:
                            v.wait_ge(scores_ready.sem, scores_ready.at(4 * (n - 1) - 2))
                        e, dq, dk = halves(E, m), halves(qd[:, n % 2], m), halves(kd[:, n % 2], m)
                        step(nc.vector.tensor_tensor(dq[:, :, :, 1, :], halves(q[:, :, 0:SEQ], m)[:, :, :, 1, :],
                                                     e[:, :, :, 1, :], ALU.mult))
                        step(nc.vector.tensor_tensor(dk[:, :, :, 0, :], halves(k[:, :, 0:SEQ], m)[:, :, :, 0, :],
                                                     e[:, :, :, 0, :], ALU.mult))
                        v.sem_inc(probs_ready.sem, 1)
                        probs_ready.given += 1
                        if n + 1 < len(levels):
                            exponents(n + 1)
                        for b in range(2 if i is None else 4):
                            w = b if i is None else 4 * n - 2 + b
                            v.wait_ge(scores_ready.sem, scores_ready.at(w + 1))
                            src = PS[:, w % 8, :]
                            if i is None:
                                ins = nc.vector.tensor_copy(A2[:, 4 * b:4 * b + 4, :].rearrange("p h n -> p (h n)"), src)
                            else:
                                ins = nc.vector.copy_predicated(
                                    A[:, b // 2, 4 * (b % 2):4 * (b % 2) + 4, :],
                                    bc(masks[:, i, :], 1, 4).bitcast(I32), src.rearrange("p (h n) -> p h n", h=4))
                            scores_taken.on(ins)
                    for b in range(4):
                        w = 4 * len(levels) - 2 + b
                        v.wait_ge(scores_taken.sem, scores_taken.at(w - 3))
                        v.wait_ge(scores_ready.sem, scores_ready.at(w + 1))
                        scores_taken.on(nc.vector.copy_predicated(
                            A[:, b // 2, 4 * (b % 2):4 * (b % 2) + 4, :], bc(masks[:, 7, :], 1, 4).bitcast(I32),
                            PS[:, w % 8, :].rearrange("p (h n) -> p h n", h=4)))
                    last = cum[:, :, SEQ - 1:SEQ].broadcast_to([128, HG_H, SEQ])
                    max_ready.on(nc.vector.tensor_tensor(E, last, cum, ALU.subtract))
                    v.wait_ge(exp_ready.sem, exp_ready.at(len(levels) + 1))
                    v.wait_ge(out_ready.sem, out_ready.at(1))
                    pt_ready.on(nc.vector.tensor_tensor(E, E, k[:, :, 0:SEQ], ALU.mult))

                @block.scalar
                def _(act):
                    step = stepper(act, act_step)
                    act.wait_ge(given.sem, given.at(1))
                    step(nc.scalar.activation(E, f[:, :, 0:SEQ], ACT.Ln))
                    for n in range(len(levels) + 1):
                        act.wait_ge(max_ready.sem, max_ready.at(n + 1))
                        exp_ready.on(nc.scalar.activation(E, E, ACT.Exp))
                    act.wait_ge(out_ready.sem, out_ready.at(1))
                    out_taken.on(nc.scalar.activation(hT[:, :, 0:SEQ], PS[:, :, 0:SEQ], ACT.Copy))

                @block.tensor
                def _(pe):
                    for n, (m, i) in enumerate(levels + [(0, 7)]):
                        if n < len(levels):
                            pe.wait_ge(probs_ready.sem, probs_ready.at(n + 1))
                            kk, qq = kd[:, n % 2], qd[:, n % 2]
                        else:
                            kk, qq = k, q
                        for b in range(2 if i is None else 4):
                            w = b if i is None else 4 * n - 2 + b
                            if w >= 8:
                                pe.wait_ge(scores_taken.sem, scores_taken.at(w - 7))
                            for h in range(4):
                                if i is None:
                                    hh, s, t = 4 * b + h, slice(0, 128), slice(128, 256)
                                else:
                                    hh = 4 * (b % 2) + h
                                    s = t = slice((b // 2) * 128, (b // 2) * 128 + 128)
                                ins = nc.tensor.matmul(PS[:, w % 8, h * 128:(h + 1) * 128], kk[:, hh, s], qq[:, hh, t],
                                                       start=True, stop=True)
                            scores_ready.on(ins)
                    pe.wait_ge(scores_taken.sem, scores_taken.at(4 * len(levels) + 2))
                    for h in range(HG_H):
                        hv = slice(h * 128, (h + 1) * 128)
                        nc.tensor.matmul(PS[:, h, 0:128], v_tok[:, 0, hv], A[:, 0, h, :], start=True, stop=True)
                        nc.tensor.matmul(PS[:, h, 128:256], v_tok[:, 0, hv], A2[:, h, :], start=True, stop=False)
                        ins = nc.tensor.matmul(PS[:, h, 128:256], v_tok[:, 1, hv], A[:, 1, h, :], start=False, stop=True)
                    out_ready.on(ins)
            end_stage()

            P = Place(after_A - 2048 - 1024 - 2048)
            k_tok = P(2, D)
            s_p = P(HG_H, 128)
            kt_s = P(D, rows=NB)
            P.at = after_A
            S = P(4, NB, 128)
            S_at = P.at
            vm = P(NB, 512, rows=NB)
            with nc.Block() as block:
                @block.sync
                def _(sp):
                    src = a["state_hgrn"][0].rearrange("b h k v -> k h b v")
                    for r in range(2):
                        if r:
                            sp.wait_ge(stored2.sem, stored2.at(64))
                            sp.wait_ge(out_ready.sem, out_ready.at(4))
                        for h in range(4):
                            loaded.on(sp.dma_start(S[:, h], src[:, 4 * r + h]), 16)
                        if r == 0:
                            sp.wait_ge(mm_taken.sem, mm_taken.at(6))
                            stored.on(sp.dma_start(hg_p[0, 0].rearrange("h k v -> k h v"), s_p), 16)
                        dst = hg_s[0].rearrange("b h k v -> k h b v")
                        for h in range(4):
                            sp.wait_ge(given.sem, given.at(4 * r + h + 1))
                            stored2.on(sp.dma_start(dst[:, 4 * r + h], S[:, h]), 16)
                    sp.wait_ge(stored2.sem, stored2.at(128))
                    sp.wait_ge(stored.sem, stored.at(16))

                def outer_out(pe, h):
                    pe.wait_ge(given.sem, given.at(h + 1))
                    for b in range(NB):
                        ins = nc.tensor.matmul(PS[:, 6, h * NB + b:h * NB + b + 1], S[:, h % 4, b, :],
                                               q[:, h, SEQ + b:SEQ + b + 1], start=True, stop=True)
                    out_ready.on(ins)

                @block.tensor
                def _(pe):
                    for n in range(4):
                        for x in range(4):
                            i, h = n // 2, 4 * (n % 2) + x
                            ins = nc.tensor.transpose(PS[:, n, x * 128:(x + 1) * 128], E[:, h, i * 128:(i + 1) * 128], ident)
                        mm_ready.on(ins)
                    for h in range(HG_H):
                        ins = nc.tensor.transpose(PS[0:NB, 4 + h // 4, (h % 4) * 128:(h % 4 + 1) * 128],
                                                  k[:, h, SEQ:T], ident)
                    aux_ready.on(ins)
                    pe.wait_ge(mm_taken.sem, mm_taken.at(4))
                    for h in range(HG_H):
                        hv = slice(h * 128, (h + 1) * 128)
                        o = PS[:, h // 4, (h % 4) * 128:(h % 4 + 1) * 128]
                        nc.tensor.matmul(o, k_tok[:, 0, hv], v_tok[:, 0, hv], start=True, stop=False)
                        ins = nc.tensor.matmul(o, k_tok[:, 1, hv], v_tok[:, 1, hv], start=False, stop=True)
                        if h % 4 == 3:
                            mm_ready.on(ins)
                    pe.wait_ge(aux_taken.sem, aux_taken.at(1))
                    for h in range(HG_H):
                        r = h // 4
                        if h % 4 == 0:
                            pe.wait_ge(imp_ready.sem, imp_ready.at(r + 1))
                        for x in range(2):
                            i = 2 * h + x
                            if i >= 2:
                                pe.wait_ge(pt_taken.sem, pt_taken.at(i - 1))
                            pt_ready.on(nc.tensor.matmul(
                                PS[:, 2 + i % 2, :], kt_s[:, h * 128:(h + 1) * 128],
                                vm[:, 4 * x:4 * x + 4, (h % 4) * 128:(h % 4 + 1) * 128], start=True, stop=True))
                        if h:
                            outer_out(pe, h - 1)
                    outer_out(pe, HG_H - 1)

                @block.vector
                def _(v):
                    step = stepper(v, dve_step)
                    for n in range(4):
                        v.wait_ge(mm_ready.sem, mm_ready.at(n + 1))
                        mm_taken.on(nc.vector.tensor_copy(k_tok[:, n // 2, (n % 2) * 512:(n % 2 + 1) * 512], PS[:, n, :]))
                    v.wait_ge(aux_ready.sem, aux_ready.at(1))
                    aux_taken.on(nc.vector.tensor_copy(kt_s, PS[0:NB, 4:6, :].rearrange("p a n -> p (a n)")))
                    for n in range(2):
                        v.wait_ge(mm_ready.sem, mm_ready.at(5 + n))
                        mm_taken.on(nc.vector.tensor_copy(s_p[:, 4 * n:4 * n + 4, :].rearrange("p h n -> p (h n)"),
                                                          PS[:, n, :]))
                    for r in range(2):
                        if r:
                            v.wait_ge(pt_ready.sem, pt_ready.at(8))
                        vs = v_tok[0:NB, 2, r * 512:(r + 1) * 512]
                        for b in range(NB):
                            ins = nc.vector.tensor_scalar_mul(vm[:, b, :], vs, ident[0:NB, b:b + 1])
                        imp_ready.on(ins)
                        v.wait_ge(loaded.sem, loaded.at(64 * (r + 1)))
                        for h in range(4):
                            hh = 4 * r + h
                            for x in range(2):
                                i = 2 * hh + x
                                v.wait_ge(pt_ready.sem, pt_ready.at(i + 1))
                                for y in range(4):
                                    b = 4 * x + y
                                    ins = nc.vector.scalar_tensor_tensor(
                                        S[:, h, b, :], S[:, h, b, :], f[:, hh, SEQ + b:SEQ + b + 1],
                                        PS[:, 2 + i % 2, y * 128:(y + 1) * 128], ALU.mult, ALU.add)
                                step(ins)
                                v.sem_inc(pt_taken.sem, 1)
                                pt_taken.given += 1
                            v.sem_inc(given.sem, 1)
                            given.given += 1
                    v.wait_ge(out_ready.sem, out_ready.at(HG_H))
                    step(nc.vector.tensor_copy(hT[:, :, SEQ:T], PS[:, 6, 0:64].rearrange("p (h b) -> p h b", h=HG_H)))
            end_stage()

            with nc.Block() as block:
                @block.scalar
                def _(act):
                    for h in range(HG_H):
                        given.on(nc.scalar.activation(mT[:, h, :], hT[:, h, :], ACT.Square))
                    for h in range(HG_H):
                        act.wait_ge(mm_ready.sem, mm_ready.at(h + 1))
                        act_step.on(nc.scalar.activation(mT[:, h, :], PS[:, h, 0:T], ACT.Ln, bias=eps[:, :],
                                                         scale=1.0 / 128))
                    act.wait_ge(act_step.sem, act_step.at(HG_H))
                    for h in range(HG_H):
                        exp_ready.on(nc.scalar.activation(mT[:, h, :], mT[:, h, :], ACT.Exp, scale=-0.5))

                @block.tensor
                def _(pe):
                    for h in range(HG_H):
                        pe.wait_ge(given.sem, given.at(h + 1))
                        mm_ready.on(nc.tensor.matmul(PS[:, h, 0:T], ones[:, 0:128], mT[:, h, :], start=True, stop=True))

                @block.vector
                def _(v):
                    step = stepper(v, dve_step)
                    step(nc.vector.tensor_scalar_mul(g, g, hg_gain))
                    for h in range(HG_H):
                        v.wait_ge(given.sem, given.at(h + 1))
                        step(nc.vector.tensor_tensor(hT[:, h, :], hT[:, h, :], g[:, h, :], ALU.mult))
                        v.wait_ge(exp_ready.sem, exp_ready.at(h + 1))
                        step(nc.vector.tensor_tensor(hT[:, h, :], hT[:, h, :], mT[:, h, :], ALU.mult))
            end_stage()
            stage_project(hT, 1)

        state_in = [signal(f"state_in{i}") for i in range(2)]
        def mixer_ssd(l):
            P = Place()
            z = P(ZT, T)
            raw_at = P.at
            raw = P(CT, T)
            xb_at = P.at
            xb = P(CT, T)
            dt = P(T, rows=32)
            cum = P(T, rows=32)
            dec = P(T, rows=32)
            hx = P(ZT, 17)
            tok = P(3, 2, 32)
            tail = P.at
            prev = P(CT, 3 * NB)
            tmp = P(CT, NB)
            wdt = P(8, 32)
            absx = P(T, rows=32)
            P = Place(xb_at)
            prev_tok = P(CONV, rows=3 * NB)
            conv_tok = P(CONV, rows=11)

            def take(u, m, ps, rows):
                if u < 4:
                    return nc.scalar.activation(z[:, 4 * u + m, :], ps, ACT.Silu)
                return nc.scalar.activation(raw[:, 4 * (u - 4) + m, :], ps, ACT.Copy)

            def sync_extra(sp):
                loaded.on(sp.dma_start(wdt, a["ssd_w_in"][0].rearrange("(k p) n -> p k n", p=128)
                                       [:, :, SSD_I + CONV:]), 16)
                loaded.on(sp.dma_start(prev_tok, a["state_ssd_conv"][0].rearrange("b i c -> (b i) c")), 16)
                for i in range(2):
                    stored2.on(sp.dma_start(conv_s[0, :, i], a["state_ssd_conv"][0, :, i + 1]), 16)

            def tensor_extra(pe):
                pe.wait_ge(loaded.sem, loaded.at(32))
                for k in range(8):
                    ins = nc.tensor.matmul(PS[0:32, 4, 0:T], wdt[:, k, :], hT[:, k, :], start=k == 0, stop=k == 7)
                aux_ready.on(ins)
                for t in range(CT):
                    ins = nc.tensor.transpose(PS[:, 5 + t // 16, (t % 16) * 24:(t % 16 + 1) * 24],
                                              prev_tok[:, t * 128:(t + 1) * 128], ident[0:24, 0:24])
                    if t % 16 == 15:
                        aux_ready.on(ins)

            def scalar_extra(act):
                act.wait_ge(aux_ready.sem, aux_ready.at(1))
                nc.scalar.activation(dt, PS[0:32, 4, 0:T], ACT.Identity, bias=col32[:, 0:1])
                for n in range(2):
                    act.wait_ge(aux_ready.sem, aux_ready.at(2 + n))
                    nc.scalar.activation(prev[:, 16 * n:16 * n + 16, :].rearrange("p t i -> p (t i)"),
                                         PS[:, 5 + n, 0:384], ACT.Copy)

            stage_in(l, None, ["fm"] * 12, take, dict(sync=sync_extra, tensor=tensor_extra, scalar=scalar_extra))

            with nc.Block() as block:
                @block.tensor
                def _(pe):
                    for n in range(8):
                        for x in range(4):
                            ins = nc.tensor.transpose(PS[0:11, n, x * 128:(x + 1) * 128], raw[:, 4 * n + x, SEQ - 3:T], ident)
                        mm_ready.on(ins)

                @block.vector
                def _(v):
                    for n in range(8):
                        v.wait_ge(mm_ready.sem, mm_ready.at(n + 1))
                        mm_taken.on(nc.vector.tensor_copy(conv_tok[:, n * 512:(n + 1) * 512], PS[0:11, n, :]))

                @block.sync
                def _(sp):
                    sp.wait_ge(mm_taken.sem, mm_taken.at(8))
                    stored.on(sp.dma_start(conv_p[0, 0], conv_tok[0:3, :]), 16)
                    stored.on(sp.dma_start(conv_s[0, :, 2], conv_tok[3:11, :]), 16)
                    sp.wait_ge(stored.sem, stored.at(32))
            end_stage()

            with nc.Block() as block:
                @block.scalar
                def _(act):
                    for t in range(CT):
                        given.on(nc.scalar.activation(xb[:, t, 0:SEQ], raw[:, t, 0:SEQ], ACT.Identity,
                                                      bias=conv_b[:, t:t + 1], scale=conv_w[:, 3, t:t + 1]))
                    act.wait_ge(max_ready.sem, max_ready.at(1))
                    act_step.on(nc.scalar.activation(absx, absx, ACT.Exp, scale=-1.0))
                    act.wait_ge(act_step.sem, act_step.at(1))
                    act_step.on(nc.scalar.activation(absx, absx, ACT.Ln, bias=ones[0:32, 0:1]))
                    act.wait_ge(max_ready.sem, max_ready.at(2))
                    nc.scalar.activation(dec[:, 0:SEQ], cum[:, 0:SEQ], ACT.Exp, scale=-1.0, bias=cum[:, SEQ - 1:SEQ])
                    nc.scalar.activation(dec[:, SEQ:T], cum[:, SEQ:T], ACT.Exp)
                    for t in range(CT):
                        act.wait_ge(taken.sem, taken.at(t + 1))
                        nc.scalar.activation(xb[:, t, :], xb[:, t, :], ACT.Silu)

                @block.vector
                def _(v):
                    step = stepper(v, dve_step)
                    max_ready.on(nc.vector.scalar_tensor_tensor(absx, dt, -1.0, dt, ALU.mult, ALU.max))
                    s = xb[:, :, SEQ:T]
                    step(nc.vector.tensor_tensor(s, raw[:, :, SEQ:T], bc(conv_w[:, 3], 2, NB), ALU.mult))
                    step(nc.vector.tensor_tensor(s, s, bc(conv_b, 2, NB), ALU.add))
                    for i in range(3):
                        step(nc.vector.tensor_tensor(tmp, prev[:, :, i::3], bc(conv_w[:, i], 2, NB), ALU.mult))
                        step(nc.vector.tensor_tensor(s, s, tmp, ALU.add))
                    v.wait_ge(act_step.sem, act_step.at(2))
                    step(nc.vector.tensor_scalar_max(dt, dt, 0.0))
                    step(nc.vector.tensor_tensor(dt, dt, absx, ALU.add))
                    step(nc.vector.tensor_scalar_mul(absx, dt, col32[:, 1:2]))
                    nc.vector.tensor_copy(cum[:, SEQ:T], absx[:, SEQ:T])
                    max_ready.on(nc.vector.tensor_tensor_scan(cum[:, 0:SEQ], ones[0:32, :], absx[:, 0:SEQ], 0.0,
                                                              ALU.mult, ALU.add))
                    for t in range(CT):
                        v.wait_ge(given.sem, given.at(t + 1))
                        for i in (2, 1, 0):
                            d = 3 - i
                            o = xb[:, t, d:SEQ]
                            step(nc.vector.scalar_tensor_tensor(o, raw[:, t, 0:SEQ - d], conv_w[:, i, t:t + 1], o,
                                                                ALU.mult, ALU.add))
                        v.sem_inc(taken.sem, 1)
                        taken.given += 1
            end_stage()

            P = Place(raw_at)
            xdt = P(2, SSD_I)
            b_tok = P(2, SSD_G * SSD_N)
            bc_tok = P(2 * SSD_G * SSD_N, rows=NB)
            with nc.Block() as block:
                @block.tensor
                def _(pe):
                    for j, src in enumerate((dt, cum, dec)):
                        for i in range(2):
                            nc.tensor.transpose(PS[:, 7, (2 * j + i) * 32:(2 * j + i + 1) * 32],
                                                src[:, i * 128:(i + 1) * 128], ident[0:32, 0:32])
                    for j in range(ZT):
                        for e in range(2):
                            for c, src in ((0, dec[:, SEQ:T]), (8, dt[:, SEQ:T]), (16, col32[:, 2:3])):
                                n = src.shape[1]
                                ins = nc.tensor.matmul(
                                    PS[64 * e:64 * e + 64, 6, j * 17 + c:j * 17 + c + n],
                                    ident[0:32, 2 * j + e:2 * j + e + 1].broadcast_to([32, 64]), src,
                                    start=True, stop=True)
                    aux_ready.on(ins)
                    for n in range(16):
                        if n >= 4:
                            pe.wait_ge(mm_taken.sem, mm_taken.at(n - 3))
                        for x in range(4):
                            if n < 12:
                                i, t = n % 2, (n // 2) * 4 + x
                                o, src = PS[:, n % 4, x * 128:(x + 1) * 128], xb[:, t, i * 128:(i + 1) * 128]
                            else:
                                t = ZT + (n - 12) * 4 + x
                                o, src = PS[0:NB, n % 4, x * 128:(x + 1) * 128], xb[:, t, SEQ:T]
                            ins = nc.tensor.transpose(o, src, ident)
                        mm_ready.on(ins)

                @block.vector
                def _(v):
                    step = stepper(v, dve_step)
                    v.wait_ge(aux_ready.sem, aux_ready.at(1))
                    step(nc.vector.tensor_copy(tok.rearrange("p j i h -> p (j i h)") if len(tok.shape) == 4 else
                                               tok.rearrange("p j i -> p (j i)"), PS[:, 7, 0:192]))
                    step(nc.vector.tensor_copy(hx.rearrange("p j c -> p (j c)"), PS[:, 6, 0:ZT * 17]))
                    for n in range(16):
                        v.wait_ge(mm_ready.sem, mm_ready.at(n + 1))
                        c = (n // 2) * 512
                        if n < 8:
                            ins = nc.vector.tensor_tensor(
                                xdt[:, n % 2, c:c + 512].rearrange("p (h d) -> p h d", d=64),
                                PS[:, n % 4, :].rearrange("p (h d) -> p h d", d=64),
                                bc(tok[:, 0, n % 2, (n // 2) * 8:(n // 2) * 8 + 8], 2, 64), ALU.mult)
                        elif n < 12:
                            ins = nc.vector.tensor_copy(b_tok[:, n % 2, c - 2048:c - 1536], PS[:, n % 4, :])
                        else:
                            ins = nc.vector.tensor_copy(bc_tok[:, (n - 12) * 512:(n - 11) * 512], PS[0:NB, n % 4, :])
                        mm_taken.on(ins)
            end_stage()

            P = Place(tail)
            cb = P(384)
            W = [P(4, 384), mT[:, :, :].rearrange("p t n -> p (t n)")[:, 0:1536].rearrange("p (h n) -> p h n", h=4)]
            with nc.Block() as block:
                @block.tensor
                def _(pe):
                    def products(g):
                        b = 4 * (g % 2)
                        if g >= 2:
                            pe.wait_ge(scores_taken.sem, scores_taken.at(g - 1))
                        nc.tensor.matmul(PS[:, b, 0:SEQ], xb[:, 16 + g, 0:128], xb[:, 24 + g, 0:SEQ], start=True, stop=True)
                        nc.tensor.matmul(PS[:, b, SEQ:384], xb[:, 16 + g, 128:SEQ], xb[:, 24 + g, 128:SEQ],
                                         start=True, stop=True)
                        for h in range(4):
                            ins = nc.tensor.matmul(PS[:, b + 1 + h // 2, (h % 2) * SEQ:(h % 2 + 1) * SEQ],
                                                   ident[0:32, 4 * g + h:4 * g + h + 1].broadcast_to([32, 128]),
                                                   cum[:, 0:SEQ], start=True, stop=True)
                        scores_ready.on(ins)

                    products(0)
                    for g in range(SSD_G):
                        if g + 1 < SSD_G:
                            products(g + 1)
                        pe.wait_ge(probs_ready.sem, probs_ready.at(g + 1))
                        if g >= 2:
                            pe.wait_ge(out_taken.sem, out_taken.at(g - 1))
                        for h in range(4):
                            hh = slice((4 * g + h) * 64, (4 * g + h + 1) * 64)
                            o = PS[64 * (h % 2):64 * (h % 2) + 64, 3 + 4 * (g % 2), (h // 2) * SEQ:(h // 2 + 1) * SEQ]
                            nc.tensor.matmul(o, xdt[:, 0, hh], W[g % 2][:, h, 0:SEQ], start=True, stop=False)
                            ins = nc.tensor.matmul(o[:, 128:SEQ], xdt[:, 1, hh], W[g % 2][:, h, SEQ:384],
                                                   start=False, stop=True)
                        out_ready.on(ins)

                @block.vector
                def _(v):
                    step = stepper(v, dve_step)

                    def exponents(g):
                        b, w = 4 * (g % 2), W[g % 2]
                        v.wait_ge(scores_ready.sem, scores_ready.at(g + 1))
                        if g >= 2:
                            v.wait_ge(out_ready.sem, out_ready.at(g - 1))
                        for h in range(4):
                            ps = PS[:, b + 1 + h // 2, (h % 2) * SEQ:(h % 2 + 1) * SEQ]
                            hh = 4 * g + h
                            nc.vector.tensor_scalar(w[:, h, 0:SEQ], ps, tok[:, 1, 0, hh:hh + 1], 0.0, ALU.subtract, ALU.min)
                            ins = nc.vector.tensor_scalar(w[:, h, SEQ:384], ps[:, 128:SEQ], tok[:, 1, 1, hh:hh + 1], 0.0,
                                                          ALU.subtract, ALU.min)
                        max_ready.on(ins)

                    def gate(g):
                        v.wait_ge(out_ready.sem, out_ready.at(g + 1))
                        for x in range(2):
                            j = 2 * g + x
                            ins = nc.vector.scalar_tensor_tensor(
                                xb[:, j, 0:SEQ], xb[:, j, 0:SEQ], hx[:, j, 16:17],
                                PS[:, 3 + 4 * (g % 2), x * SEQ:(x + 1) * SEQ], ALU.mult, ALU.add)
                        out_taken.on(ins)

                    exponents(0)
                    for g in range(SSD_G):
                        step(nc.vector.tensor_tensor(cb, PS[:, 4 * (g % 2), 0:384], con("causal_mul"), ALU.mult))
                        v.sem_inc(scores_taken.sem, 1)
                        scores_taken.given += 1
                        if g + 1 < SSD_G:
                            exponents(g + 1)
                        v.wait_ge(exp_ready.sem, exp_ready.at(g + 1))
                        probs_ready.on(nc.vector.tensor_tensor(W[g % 2], W[g % 2], bc(cb, 1, 4), ALU.mult))
                        v.wait_ge(probs_ready.sem, probs_ready.at(g + 1))
                        if g:
                            gate(g - 1)
                    gate(SSD_G - 1)
                    for i in range(2):
                        x = xdt[:, i, :].rearrange("p (h d) -> p h d", d=64)
                        given.on(nc.vector.tensor_tensor(x, x, bc(tok[:, 2, i, :], 2, 64), ALU.mult))

                @block.scalar
                def _(act):
                    for g in range(SSD_G):
                        act.wait_ge(max_ready.sem, max_ready.at(g + 1))
                        exp_ready.on(nc.scalar.activation(W[g % 2], W[g % 2], ACT.Exp))
            end_stage()

            P = Place(tail)
            s_p = P(ZT, 128)
            dx = P(ZT, NB)
            ys = P(ZT, NB)
            P = Place(raw_at)
            S = P(2, ZT, 128)
            tm = P(ZT, 128)
            assert P.at <= raw_at + 6144
            state = a["state_ssd"][0].rearrange("b (j e) p n -> b (e p) j n", e=2)
            state_out = ssd_s[0].rearrange("b (j e) p n -> b (e p) j n", e=2)
            with nc.Block() as block:
                @block.tensor
                def _(pe):
                    for j in range(ZT):
                        o = PS[:, j // 4, (j % 4) * 128:(j % 4 + 1) * 128]
                        for i in range(2):
                            ins = nc.tensor.matmul(o, xdt[:, i, j * 128:(j + 1) * 128],
                                                   b_tok[:, i, (j // 2) * 128:(j // 2 + 1) * 128],
                                                   start=i == 0, stop=i == 1)
                        if j % 4 == 3:
                            mm_ready.on(ins)
                    for b in range(NB):
                        if b == 0:
                            pe.wait_ge(mm_taken.sem, mm_taken.at(4))
                        if b >= 2:
                            pe.wait_ge(pt_taken.sem, pt_taken.at(b - 1))
                        for x in range(4):
                            ins = nc.tensor.matmul(PS[:, 4 * (b % 2) + x, :], ident[0:NB, b:b + 1].broadcast_to([NB, 128]),
                                                   bc_tok[:, x * 512:(x + 1) * 512], start=True, stop=True)
                        pt_ready.on(ins)

                @block.scalar
                def _(act):
                    for n in range(4):
                        act.wait_ge(mm_ready.sem, mm_ready.at(n + 1))
                        mm_taken.on(nc.scalar.activation(s_p[:, 4 * n:4 * n + 4, :].rearrange("p j n -> p (j n)"),
                                                         PS[:, n, :], ACT.Copy))

                @block.sync
                def _(sp):
                    sp.wait_ge(mm_ready.sem, mm_ready.at(4))
                    for b in range(NB):
                        if b >= 2:
                            sp.wait_ge(stored2.sem, stored2.at(16 * (b - 1)))
                            sp.wait_ge(pt_taken.sem, pt_taken.at(b - 1))
                        state_in[b % 2].on(sp.dma_start(S[:, b % 2], state[b]), 16)
                        if b == 0:
                            sp.wait_ge(mm_taken.sem, mm_taken.at(4))
                            stored.on(sp.dma_start(ssd_p[0, 0].rearrange("(j e) p n -> (e p) j n", e=2), s_p), 16)
                        else:
                            sp.wait_ge(given.sem, given.at(b))
                            stored2.on(sp.dma_start(state_out[b - 1], S[:, (b - 1) % 2]), 16)
                    sp.wait_ge(given.sem, given.at(NB))
                    stored2.on(sp.dma_start(state_out[NB - 1], S[:, (NB - 1) % 2]), 16)
                    sp.wait_ge(stored2.sem, stored2.at(16 * NB))
                    sp.wait_ge(stored.sem, stored.at(16))

                @block.vector
                def _(v):
                    step = stepper(v, dve_step)
                    xs = xb[:, 0:ZT, SEQ:T]
                    step(nc.vector.tensor_tensor(dx, hx[:, :, 8:16], xs, ALU.mult))
                    for b in range(NB):
                        s = S[:, b % 2]
                        v.wait_ge(state_in[b % 2].sem, state_in[b % 2].at(16 * (b // 2 + 1)))
                        v.wait_ge(pt_ready.sem, pt_ready.at(b + 1))
                        step(nc.vector.tensor_tensor(s, s, hx[:, :, b:b + 1].broadcast_to([128, ZT, 128]), ALU.mult))
                        ps = PS[:, 4 * (b % 2):4 * (b % 2) + 4, :].rearrange("p x n -> p (x n)")
                        split = lambda x: x.rearrange("p (g e) n -> p g e n", e=2)
                        bb = bc(ps[:, 0:1024].rearrange("p (g n) -> p g n", n=128), 2, 2)
                        cc = bc(ps[:, 1024:2048].rearrange("p (g n) -> p g n", n=128), 2, 2)
                        step(nc.vector.tensor_tensor(split(tm), bb, split(dx[:, :, b:b + 1]).broadcast_to([128, 8, 2, 128]),
                                                     ALU.mult))
                        step(nc.vector.tensor_tensor(s, s, tm, ALU.add))
                        v.sem_inc(given.sem, 1)
                        given.given += 1
                        step(nc.vector.tensor_tensor(split(tm), split(s), cc, ALU.mult))
                        v.sem_inc(pt_taken.sem, 1)
                        pt_taken.given += 1
                        step(nc.vector.tensor_reduce(ys[:, :, b:b + 1], tm, AX.X, ALU.add))
                    step(nc.vector.tensor_tensor(xs, xs, hx[:, :, 16:17].broadcast_to([128, ZT, NB]), ALU.mult))
                    step(nc.vector.tensor_tensor(xs, xs, ys, ALU.add))
            end_stage()

            P = Place(raw_at)
            sq = P(ZT, T)
            rs = P(SSD_G, T)
            with nc.Block() as block:
                @block.vector
                def _(v):
                    step = stepper(v, dve_step)
                    for g in range(SSD_G):
                        x = xb[:, 2 * g:2 * g + 2, :]
                        given.on(nc.vector.tensor_tensor(x, x, z[:, 2 * g:2 * g + 2, :], ALU.mult))
                    for g in range(SSD_G):
                        v.wait_ge(exp_ready.sem, exp_ready.at(g + 1))
                        for j in (2 * g, 2 * g + 1):
                            nc.vector.scalar_tensor_tensor(xb[:, j, :], xb[:, j, :], ssd_gain[:, j:j + 1], rs[:, g, :],
                                                           ALU.mult, ALU.mult)

                @block.scalar
                def _(act):
                    for g in range(SSD_G):
                        act.wait_ge(given.sem, given.at(g + 1))
                        taken.on(nc.scalar.activation(sq[:, 2 * g:2 * g + 2, :], xb[:, 2 * g:2 * g + 2, :], ACT.Square))
                    for g in range(SSD_G):
                        act.wait_ge(mm_ready.sem, mm_ready.at(g + 1))
                        act_step.on(nc.scalar.activation(rs[:, g, :], PS[:, g, 0:T], ACT.Ln, bias=eps[:, :],
                                                         scale=1.0 / 256))
                    act.wait_ge(act_step.sem, act_step.at(SSD_G))
                    for g in range(SSD_G):
                        exp_ready.on(nc.scalar.activation(rs[:, g, :], rs[:, g, :], ACT.Exp, scale=-0.5))

                @block.tensor
                def _(pe):
                    for g in range(SSD_G):
                        pe.wait_ge(taken.sem, taken.at(g + 1))
                        nc.tensor.matmul(PS[:, g, 0:T], ones[:, 0:128], sq[:, 2 * g, :], start=True, stop=False)
                        mm_ready.on(nc.tensor.matmul(PS[:, g, 0:T], ones[:, 0:128], sq[:, 2 * g + 1, :],
                                                     start=False, stop=True))
            end_stage()
            stage_project(xb, 2)

        stage_prepare()
        stage_rows()
        stage_ada(0)
        for l in range(DEPTH):
            stage_norm(l, 0)
            (mixer_nsa, mixer_hgrn, mixer_ssd)[l % 3](l)
            stage_norm(l, 1)
            stage_norm(l, 2)
            stage_mlp(l)
            stage_norm(l, 3)
        stage_output()


_OUTS = [(1, SEQ, D), (NB, 1, D), (2, 1, SEQ, 4, KV, HD), (2, NB, 1, 4, KV, HD), (2, 1, SEQ, 2, KV, HD),
         (2, NB, WIN, 2, KV, HD), (1, 1, HG_H, 128, 128), (1, NB, HG_H, 128, 128),
         (1, 1, SSD_H, SSD_P, SSD_N), (1, NB, SSD_H, SSD_P, SSD_N), (1, 1, 3, CONV), (1, NB, 3, CONV)]
_INS = ['x_prompt', 'x_sample', 'cache_nsa_kv', 'cache_nsa_win', 'state_hgrn', 'state_ssd', 'state_ssd_conv',
        'page_table', 'c_prompt', 'c_sample', 'rel_bias', 'hgrn_lower_bounds', 'w_ada', 'b_ada', 'norm_gains',
        'w_mlp_in', 'w_mlp_out', 'nsa_w_in', 'nsa_cmp_pos', 'nsa_cmp_w1', 'nsa_cmp_w2', 'nsa_w_out',
        'hg_w_in', 'hg_norm', 'hg_w_out', 'ssd_w_in', 'ssd_conv_w', 'ssd_conv_b', 'ssd_dt_bias', 'ssd_a_log',
        'ssd_d', 'ssd_norm', 'ssd_w_out']


def kernel(**inputs):
    import concourse.bacc as bacc
    from concourse.bass_utils import run_bass_kernel_spmd

    nc = bacc.Bacc("TRN2", target_bir_lowering=False, num_devices=1)
    arrays, args = {}, {}
    for name in _INS:
        arr = np.ascontiguousarray(inputs[name])
        arrays[f"in_{name}"] = arr
        args[name] = nc.dram_tensor(f"in_{name}", arr.shape, mybir.dt.from_np(arr.dtype),
                                    kind="ExternalInput").ap()
    consts = []
    for name, arr in (("wide", WIDE), ("narrow", NARROW)):
        arrays[f"const_{name}"] = np.ascontiguousarray(arr)
        consts.append(nc.dram_tensor(f"const_{name}", arr.shape, F32, kind="ExternalInput").ap())
    outs = [nc.dram_tensor(f"out_{i}", s, F32, kind="ExternalOutput").ap() for i, s in enumerate(_OUTS)]
    hybrid_trunk(nc, args, outs, consts)
    r = run_bass_kernel_spmd(nc, [arrays], core_ids=[0])
    return tuple(r.results[0][f"out_{i}"] for i in range(len(_OUTS)))
```
